# Optimizing a Trainium2 kernel written in Bass

```python
import math
import functools
import jax
import jax.numpy as jnp
from jax import lax
import numpy as np

D_MODEL = 1024
BATCH = 1
SEQ = 512
DEPTH = 1
DEC_BATCH = 8
DEC_SEQ = 1
PAST_LEN = 2048
PAGE_SIZE = 128

HEAD_DIM = 64
GROUP_WIDTH = D_MODEL // 4
A_HEADS = GROUP_WIDTH // HEAD_DIM
NSA_HEADS = GROUP_WIDTH // HEAD_DIM
DSA_HEADS = GROUP_WIDTH // HEAD_DIM
CONV_CH = GROUP_WIDTH
RWKV_W_RANK = 32
RWKV_A_RANK = 32
RWKV_G_RANK = 64
RWKV_DECAY_SCALE = 0.606531
RWKV_GN_EPS = 64e-5
NSA_CMP_BLOCK = 32
NSA_CMP_HIDDEN = 128
NSA_SEL_BLOCK = 64
NSA_TOPN = 16
NSA_LOCAL_BLOCKS = 2
NSA_WINDOW = 512
DSA_TOPK = 256
IDX_HEADS = 4
IDX_DIM = 32
CONV_K = 3
N_EXPERTS = 32
TOP_K = 4
EXPERT_FF = D_MODEL
SWIGLU_LIMIT = 7.0
SWIGLU_ALPHA = 1.702
MOE_MAX_BLOCK = 256
Q_BLOCK = 128
DN_ALPHA = (2 * DEPTH) ** 0.25
DN_BETA = (8 * DEPTH) ** -0.25
NEG_INF = -1e30
FORCE_SCORE = 1e4
A_COLS = 3 * GROUP_WIDTH + RWKV_W_RANK + RWKV_A_RANK + RWKV_G_RANK
B_COLS = GROUP_WIDTH + 6 * HEAD_DIM + 3 * NSA_HEADS
C_COLS = GROUP_WIDTH + 2 * HEAD_DIM + IDX_HEADS * IDX_DIM + IDX_DIM + IDX_HEADS
D_COLS = 3 * CONV_CH
IN_COLS = A_COLS + B_COLS + C_COLS + D_COLS

kernel_name = 'hybrid_rwkv7_nsa_dsa_shortconv_moe_step'

def _take(z, sizes):
    offs = np.cumsum([0] + list(sizes))
    return [z[..., int(offs[i]):int(offs[i + 1])] for i in range(len(sizes))]

def _layernorm(x, g=None, b=None, eps=1e-5):
    xf = x.astype(jnp.float32)
    mu = jnp.mean(xf, axis=-1, keepdims=True)
    var = jnp.mean(jnp.square(xf - mu), axis=-1, keepdims=True)
    y = (xf - mu) * lax.rsqrt(var + eps)
    if g is not None:
        y = y * g.astype(jnp.float32) + b.astype(jnp.float32)
    return y.astype(x.dtype)

def _masked_softmax(s, valid):
    p = jax.nn.softmax(jnp.where(valid, s, NEG_INF), axis=-1)
    return jnp.where(valid, p, 0.0)

def _alibi_slopes(n):
    return 2.0 ** (-8.0 * jnp.arange(1, n + 1, dtype=jnp.float32) / n)

def _rows_fetch(src):
    def fetch(pos):
        b = pos.shape[0]
        flat = jnp.clip(pos.reshape(b, -1), 0, src.shape[1] - 1)
        return src[jnp.arange(b)[:, None], flat].reshape(pos.shape + src.shape[2:])
    return fetch

def _paged_fetch(pool, page_table, new_rows):
    n_past = page_table.shape[1] * PAGE_SIZE
    n_new = new_rows.shape[1]

    def fetch(pos):
        b = pos.shape[0]
        flat = pos.reshape(b, -1)
        bi = jnp.arange(b)[:, None]
        pc = jnp.clip(flat, 0, n_past - 1)
        past = pool[page_table[bi, pc // PAGE_SIZE], pc % PAGE_SIZE]
        new = new_rows[bi, jnp.clip(flat - n_past, 0, n_new - 1)].astype(past.dtype)
        is_past = (flat < n_past).reshape(flat.shape + (1,) * (past.ndim - 2))
        return jnp.where(is_past, past, new).reshape(pos.shape + past.shape[2:])
    return fetch

def _rwkv_mixer(za, shift_prev, s0, lp):
    b, t, _ = za.shape
    f32 = jnp.float32
    z_prev = jnp.concatenate([shift_prev[:, None].astype(za.dtype), za[:, :-1]], axis=1)
    zs = za + lp['rwkv_mu'] * (z_prev - za)
    r, k, v, w_lo, a_lo, g_lo = _take(zs, [GROUP_WIDTH] * 3 + [RWKV_W_RANK, RWKV_A_RANK, RWKV_G_RANK])
    decay = jnp.exp(-RWKV_DECAY_SCALE * jax.nn.sigmoid((lp['rwkv_w0'] + jnp.tanh(w_lo) @ lp['rwkv_w2']).astype(f32)))
    a = jax.nn.sigmoid((lp['rwkv_a0'] + a_lo @ lp['rwkv_a2']).astype(f32))
    g = jax.nn.sigmoid(g_lo) @ lp['rwkv_g2']
    heads = lambda u: u.astype(f32).reshape(b, t, A_HEADS, HEAD_DIM)
    r, k, v, decay, a = heads(r), heads(k), heads(v), heads(decay), heads(a)
    kk = k * lp['rwkv_kk']
    kk = kk / jnp.maximum(jnp.sqrt(jnp.sum(kk * kk, axis=-1, keepdims=True)), 1e-12)
    k = k * (1.0 + (a - 1.0) * lp['rwkv_ka'])

    def step(s, inp):
        r_t, k_t, v_t, w_t, kk_t, a_t = inp
        s = (s * w_t[:, :, None, :]
             - jnp.einsum('bhvk,bhk->bhv', s, kk_t)[..., None] * (kk_t * a_t)[:, :, None, :]
             + v_t[..., None] * k_t[:, :, None, :])
        return s, jnp.einsum('bhvk,bhk->bhv', s, r_t)

    xs = tuple(jnp.swapaxes(u, 0, 1) for u in (r, k, v, decay, kk, a))
    s_fin, y = lax.scan(step, s0.astype(f32), xs)
    y = jnp.swapaxes(y, 0, 1)
    mu = jnp.mean(y, axis=-1, keepdims=True)
    var = jnp.mean(jnp.square(y - mu), axis=-1, keepdims=True)
    yn = ((y - mu) * lax.rsqrt(var + RWKV_GN_EPS) * lp['rwkv_gn_g'].reshape(A_HEADS, HEAD_DIM)
          + lp['rwkv_gn_b'].reshape(A_HEADS, HEAD_DIM))
    bonus = jnp.sum(r * k * lp['rwkv_rk'], axis=-1, keepdims=True) * v
    out = (yn + bonus).reshape(b, t, GROUP_WIDTH) * g
    return out.astype(za.dtype), s_fin, za[:, -1]

def _nsa_split(zb):
    b, t, _ = zb.shape
    q, kc, ks, kw, gl = _take(zb, [GROUP_WIDTH, 2 * HEAD_DIM, 2 * HEAD_DIM, 2 * HEAD_DIM, 3 * NSA_HEADS])
    kv = lambda u: u.reshape(b, t, 2, HEAD_DIM)
    gates = jax.nn.sigmoid(gl.astype(jnp.float32)).reshape(b, t, NSA_HEADS, 3)
    return q.reshape(b, t, NSA_HEADS, HEAD_DIM), kv(kc), kv(ks), kv(kw), gates

def _nsa_compress(rows, lp):
    b, l = rows.shape[:2]
    nc = l // NSA_CMP_BLOCK
    blk = rows[:, :nc * NSA_CMP_BLOCK].astype(jnp.float32).reshape(b, nc, NSA_CMP_BLOCK, 2, HEAD_DIM) + lp['nsa_pe']
    flat = jnp.swapaxes(blk, 2, 3).reshape(b, nc, 2, NSA_CMP_BLOCK * HEAD_DIM)
    hid = jax.nn.gelu(jnp.einsum('bnci,cih->bnch', flat, lp['nsa_w1']))
    return jnp.einsum('bnch,chd->bncd', hid, lp['nsa_w2'])

def _nsa_attend(q, gates, qpos, kvc, fetch_slc, kvw, wpos, slopes, n_keys):
    f32 = jnp.float32
    b, tq = q.shape[:2]
    q = q.astype(f32) * HEAD_DIM ** -0.5
    kvc = kvc.astype(f32)
    kvw = kvw.astype(f32)
    sl = slopes[:, None, None]
    nc = kvc.shape[1]
    cend = jnp.arange(nc) * NSA_CMP_BLOCK + (NSA_CMP_BLOCK - 1)
    s_c = jnp.einsum('bqhd,bnd->bhqn', q, kvc[:, :, 0]) - sl * (qpos[:, None] - cend[None, :]).astype(f32)
    p_c = _masked_softmax(s_c, cend[None, :] <= qpos[:, None])
    o_c = jnp.einsum('bhqn,bnd->bqhd', p_c, kvc[:, :, 1])
    ratio = NSA_SEL_BLOCK // NSA_CMP_BLOCK
    n_sel = -(-n_keys // NSA_SEL_BLOCK)
    imp = jnp.pad(p_c.sum(1), ((0, 0), (0, 0), (0, n_sel * ratio - nc))).reshape(b, tq, n_sel, ratio).sum(-1)
    blk = jnp.arange(n_sel)[None, :]
    cur = (qpos // NSA_SEL_BLOCK)[:, None]
    forced = (blk == 0) | (blk > cur - NSA_LOCAL_BLOCKS)
    score = jnp.where(blk > cur, NEG_INF, jnp.where(forced, FORCE_SCORE, imp))
    n_top = min(NSA_TOPN, n_sel)
    _, sel = lax.top_k(score, n_top)
    kpos = (sel[..., None] * NSA_SEL_BLOCK + jnp.arange(NSA_SEL_BLOCK)).reshape(b, tq, n_top * NSA_SEL_BLOCK)
    kv_s = fetch_slc(kpos).astype(f32)
    s_s = (jnp.einsum('bqhd,bqnd->bhqn', q, kv_s[..., 0, :])
           - sl * (qpos[None, None, :, None] - kpos[:, None]).astype(f32))
    p_s = _masked_softmax(s_s, (kpos <= qpos[None, :, None])[:, None])
    o_s = jnp.einsum('bhqn,bqnd->bqhd', p_s, kv_s[..., 1, :])
    dw = qpos[:, None] - wpos[None, :]
    s_w = jnp.einsum('bqhd,bnd->bhqn', q, kvw[:, :, 0]) - sl * dw.astype(f32)
    p_w = _masked_softmax(s_w, (dw >= 0) & (dw <= NSA_WINDOW) & (wpos[None, :] >= 0))
    o_w = jnp.einsum('bhqn,bnd->bqhd', p_w, kvw[:, :, 1])
    return gates[..., 0:1] * o_c + gates[..., 1:2] * o_s + gates[..., 2:3] * o_w

def _dsa_split(zc):
    b, t, _ = zc.shape
    q, kv, qi, ki, wi = _take(zc, [GROUP_WIDTH, 2 * HEAD_DIM, IDX_HEADS * IDX_DIM, IDX_DIM, IDX_HEADS])
    return (q.reshape(b, t, DSA_HEADS, HEAD_DIM), kv.reshape(b, t, 2, HEAD_DIM),
            qi.reshape(b, t, IDX_HEADS, IDX_DIM), ki, wi)

def _dsa_attend(q, qi, wi, qpos, kidx, fetch_kv, slopes, n_keys):
    f32 = jnp.float32
    l = kidx.shape[1]
    rel = jax.nn.relu(jnp.einsum('bqhi,bsi->bqhs', qi.astype(f32), kidx.astype(f32)))
    score = jnp.einsum('bqh,bqhs->bqs', wi.astype(f32), rel)
    score = jnp.where(jnp.arange(l)[None, None, :] <= qpos[None, :, None], score, NEG_INF)
    k_sel = min(DSA_TOPK, n_keys // 4)
    _, sel = lax.top_k(score, k_sel)
    kv = fetch_kv(sel).astype(f32)
    s = (jnp.einsum('bqhd,bqnd->bhqn', q.astype(f32) * HEAD_DIM ** -0.5, kv[..., 0, :])
         - slopes[:, None, None] * (qpos[None, None, :, None] - sel[:, None]).astype(f32))
    p = _masked_softmax(s, (sel <= qpos[None, :, None])[:, None])
    return jnp.einsum('bhqn,bqnd->bqhd', p, kv[..., 1, :])

def _conv_mixer(zd, buf, conv_w):
    t = zd.shape[1]
    b_gate, c_gate, xin = _take(zd, [CONV_CH] * 3)
    ue = jnp.concatenate([buf.astype(zd.dtype), c_gate * xin], axis=1)
    y = sum(ue[:, j:j + t] * conv_w[j] for j in range(CONV_K))
    return b_gate * y, ue[:, t:]

def _moe_block_rows(n_assign):
    per_expert = max(1, n_assign // N_EXPERTS)
    return min(MOE_MAX_BLOCK, max(8, 1 << (per_expert.bit_length() - 1)))

def _moe(h, lp):
    b, t, d = h.shape
    n = b * t
    x = h.reshape(n, d)
    logits = (x @ lp['moe_wr'] + lp['moe_br']).astype(jnp.float32)
    top_v, top_e = lax.top_k(logits, TOP_K)
    gate = jax.nn.softmax(top_v, axis=-1)
    m = n * TOP_K
    blk = _moe_block_rows(m)
    cap = -(-(m + N_EXPERTS * (blk - 1)) // blk) * blk
    e_flat = top_e.reshape(m)
    order = jnp.argsort(e_flat)
    e_s = e_flat[order]
    tok_s = (jnp.arange(m, dtype=jnp.int32) // TOP_K)[order]
    g_s = gate.reshape(m)[order]
    counts = jnp.bincount(e_flat, length=N_EXPERTS)
    padded = (counts + blk - 1) // blk * blk
    pend = jnp.cumsum(padded)
    dest = (pend - padded)[e_s] + jnp.arange(m) - (jnp.cumsum(counts) - counts)[e_s]
    row_tok = jnp.zeros((cap,), jnp.int32).at[dest].set(tok_s)
    blk_exp = jnp.minimum(jnp.searchsorted(pend, jnp.arange(cap // blk) * blk, side='right'), N_EXPERTS - 1)
    wgu, bgu, wd, bd = lp['moe_wgu'], lp['moe_bgu'], lp['moe_wd'], lp['moe_bd']

    def expert_block(args):
        rows, e = args
        gu = x[rows] @ wgu[e] + bgu[e]
        gt, up = jnp.split(gu, 2, axis=-1)
        gt = jnp.minimum(gt, SWIGLU_LIMIT)
        up = jnp.clip(up, -SWIGLU_LIMIT, SWIGLU_LIMIT)
        return ((up + 1.0) * gt * jax.nn.sigmoid(SWIGLU_ALPHA * gt)) @ wd[e] + bd[e]

    out = lax.map(expert_block, (row_tok.reshape(cap // blk, blk), blk_exp)).reshape(cap, d)
    y = jnp.zeros((n, d), jnp.float32).at[tok_s].add(g_s[:, None] * out[dest].astype(jnp.float32))
    return y.reshape(b, t, d).astype(h.dtype)

def _layer(x, c, lp, mixer_fn):
    mod = jax.nn.silu(c) @ lp['w_ada'] + lp['b_ada']
    sh1, sc1, g1, sh2, sc2, g2 = [u[:, None, :] for u in jnp.split(mod, 6, axis=-1)]
    h = _layernorm(x) * (1.0 + sc1) + sh1
    mix, states = mixer_fn(h @ lp['w_in'])
    x = _layernorm(DN_ALPHA * x + g1 * (mix @ lp['w_out']), lp['ln1_g'], lp['ln1_b'])
    h = _layernorm(x) * (1.0 + sc2) + sh2
    x = _layernorm(DN_ALPHA * x + g2 * _moe(h, lp), lp['ln2_g'], lp['ln2_b'])
    return x, states

def _mixers_prompt(z, lp, sl_nsa, sl_dsa):
    b, t, _ = z.shape
    za, zb, zc, zd = _take(z, [A_COLS, B_COLS, C_COLS, D_COLS])
    ya, s_rwkv, shift = _rwkv_mixer(za, jnp.zeros((b, A_COLS), z.dtype),
                                    jnp.zeros((b, A_HEADS, HEAD_DIM, HEAD_DIM), jnp.float32), lp)
    q, kv_c, kv_s, kv_w, gates = _nsa_split(zb)
    kvc = _nsa_compress(kv_c, lp)
    fetch_s = _rows_fetch(kv_s)
    kvw_pad = jnp.pad(kv_w, ((0, 0), (NSA_WINDOW, 0), (0, 0), (0, 0)))
    qc, kv_d, qi, ki, wi = _dsa_split(zc)
    fetch_d = _rows_fetch(kv_d)
    starts = jnp.arange(t // Q_BLOCK, dtype=jnp.int32) * Q_BLOCK

    def nsa_block(q0):
        cut = lambda u: lax.dynamic_slice_in_dim(u, q0, Q_BLOCK, axis=1)
        kvw = lax.dynamic_slice_in_dim(kvw_pad, q0, NSA_WINDOW + Q_BLOCK, axis=1)
        wpos = q0 - NSA_WINDOW + jnp.arange(NSA_WINDOW + Q_BLOCK)
        return _nsa_attend(cut(q), cut(gates), q0 + jnp.arange(Q_BLOCK), kvc, fetch_s, kvw, wpos, sl_nsa, t)

    def dsa_block(q0):
        cut = lambda u: lax.dynamic_slice_in_dim(u, q0, Q_BLOCK, axis=1)
        return _dsa_attend(cut(qc), cut(qi), cut(wi), q0 + jnp.arange(Q_BLOCK), ki, fetch_d, sl_dsa, t)

    unblock = lambda o: jnp.swapaxes(o, 0, 1).reshape(b, t, GROUP_WIDTH).astype(z.dtype)
    yb = unblock(lax.map(nsa_block, starts))
    yc = unblock(lax.map(dsa_block, starts))
    yd, conv_buf = _conv_mixer(zd, jnp.zeros((b, CONV_K - 1, CONV_CH), z.dtype), lp['conv_w'])
    mix = jnp.concatenate([ya, yb, yc, yd], axis=-1)
    return mix, (s_rwkv, shift, kv_c, kv_s, kv_w[:, -min(NSA_WINDOW, t):], kv_d, ki, conv_buf)

def _mixers_sample(z, lp, sl_nsa, sl_dsa, s_rwkv, s_shift, c_nsa_cmp, c_nsa_slc, s_win,
                   c_dsa_kv, c_dsa_idx, s_conv, page_table):
    b, t, _ = z.shape
    n_past = page_table.shape[1] * PAGE_SIZE
    n_buf = s_win.shape[1]
    qpos = n_past + jnp.arange(t)
    za, zb, zc, zd = _take(z, [A_COLS, B_COLS, C_COLS, D_COLS])
    ya, s_rwkv_new, shift = _rwkv_mixer(za, s_shift, s_rwkv, lp)
    q, kv_c, kv_s, kv_w, gates = _nsa_split(zb)
    past_c = c_nsa_cmp[page_table].reshape(b, n_past, 2, HEAD_DIM)
    kvc = _nsa_compress(jnp.concatenate([past_c, kv_c.astype(past_c.dtype)], axis=1), lp)
    kvw = jnp.concatenate([s_win, kv_w.astype(s_win.dtype)], axis=1)
    wpos = n_past - n_buf + jnp.arange(n_buf + t)
    yb = _nsa_attend(q, gates, qpos, kvc, _paged_fetch(c_nsa_slc, page_table, kv_s), kvw, wpos, sl_nsa, n_past + t)
    qc, kv_d, qi, ki, wi = _dsa_split(zc)
    past_i = c_dsa_idx[page_table].reshape(b, n_past, IDX_DIM)
    ki_all = jnp.concatenate([past_i, ki.astype(past_i.dtype)], axis=1)
    yc = _dsa_attend(qc, qi, wi, qpos, ki_all, _paged_fetch(c_dsa_kv, page_table, kv_d), sl_dsa, n_past + t)
    yd, conv_buf = _conv_mixer(zd, s_conv, lp['conv_w'])
    flat = lambda o: o.reshape(b, t, GROUP_WIDTH).astype(z.dtype)
    mix = jnp.concatenate([ya, flat(yb), flat(yc), yd], axis=-1)
    return mix, (s_rwkv_new, shift, kv_c, kv_s, kvw[:, -n_buf:], kv_d, ki, conv_buf)

def setup_inputs(seed: int = 0) -> dict:
    key = jax.random.key(seed)
    keys = jax.random.split(key, 64)
    counter = iter(range(64))
    f32 = jnp.float32

    def nrm(shape, std):
        return std * jax.random.normal(keys[next(counter)], shape, f32)

    n_pages = PAST_LEN // PAGE_SIZE
    n_pool = (5 * DEC_BATCH * n_pages + 3) // 4
    n_buf = min(NSA_WINDOW, PAST_LEN)
    page_table = jax.random.permutation(keys[next(counter)], n_pool)[:DEC_BATCH * n_pages]
    page_table = page_table.reshape(DEC_BATCH, n_pages).astype(jnp.int32)
    d = D_MODEL
    return {
        'x_prompt': nrm((BATCH, SEQ, d), 1.0),
        'x_sample': nrm((DEC_BATCH, DEC_SEQ, d), 1.0),
        'state_rwkv': nrm((DEPTH, DEC_BATCH, A_HEADS, HEAD_DIM, HEAD_DIM), 0.3),
        'state_rwkv_shift': nrm((DEPTH, DEC_BATCH, A_COLS), 1.0),
        'cache_nsa_cmp': nrm((DEPTH, n_pool, PAGE_SIZE, 2, HEAD_DIM), 1.0),
        'cache_nsa_slc': nrm((DEPTH, n_pool, PAGE_SIZE, 2, HEAD_DIM), 1.0),
        'state_nsa_win': nrm((DEPTH, DEC_BATCH, n_buf, 2, HEAD_DIM), 1.0),
        'cache_dsa_kv': nrm((DEPTH, n_pool, PAGE_SIZE, 2, HEAD_DIM), 1.0),
        'cache_dsa_idx': nrm((DEPTH, n_pool, PAGE_SIZE, IDX_DIM), 1.0),
        'state_conv': nrm((DEPTH, DEC_BATCH, CONV_K - 1, CONV_CH), 1.0),
        'page_table': page_table,
        'c_prompt': nrm((BATCH, d), 1.0),
        'c_sample': nrm((DEC_BATCH, d), 1.0),
        'w_ada': nrm((DEPTH, d, 6 * d), 0.5 * d ** -0.5),
        'b_ada': nrm((DEPTH, 6 * d), 0.02),
        'w_in': nrm((DEPTH, d, IN_COLS), d ** -0.5),
        'w_out': nrm((DEPTH, d, d), DN_BETA * d ** -0.5),
        'ln1_g': 1.0 + nrm((DEPTH, d), 0.05),
        'ln1_b': nrm((DEPTH, d), 0.02),
        'ln2_g': 1.0 + nrm((DEPTH, d), 0.05),
        'ln2_b': nrm((DEPTH, d), 0.02),
        'rwkv_mu': jax.random.uniform(keys[next(counter)], (DEPTH, A_COLS), f32),
        'rwkv_w0': nrm((DEPTH, GROUP_WIDTH), 0.5),
        'rwkv_w2': nrm((DEPTH, RWKV_W_RANK, GROUP_WIDTH), RWKV_W_RANK ** -0.5),
        'rwkv_a0': nrm((DEPTH, GROUP_WIDTH), 0.5),
        'rwkv_a2': nrm((DEPTH, RWKV_A_RANK, GROUP_WIDTH), RWKV_A_RANK ** -0.5),
        'rwkv_g2': nrm((DEPTH, RWKV_G_RANK, GROUP_WIDTH), RWKV_G_RANK ** -0.5),
        'rwkv_kk': 0.85 + nrm((DEPTH, A_HEADS, HEAD_DIM), 0.05),
        'rwkv_ka': 1.0 + nrm((DEPTH, A_HEADS, HEAD_DIM), 0.05),
        'rwkv_rk': nrm((DEPTH, A_HEADS, HEAD_DIM), 0.1),
        'rwkv_gn_g': 1.0 + nrm((DEPTH, GROUP_WIDTH), 0.05),
        'rwkv_gn_b': nrm((DEPTH, GROUP_WIDTH), 0.02),
        'nsa_pe': nrm((DEPTH, NSA_CMP_BLOCK, 2, HEAD_DIM), 0.02),
        'nsa_w1': nrm((DEPTH, 2, NSA_CMP_BLOCK * HEAD_DIM, NSA_CMP_HIDDEN), (NSA_CMP_BLOCK * HEAD_DIM) ** -0.5),
        'nsa_w2': nrm((DEPTH, 2, NSA_CMP_HIDDEN, HEAD_DIM), NSA_CMP_HIDDEN ** -0.5),
        'conv_w': nrm((DEPTH, CONV_K, CONV_CH), 0.5),
        'moe_wr': nrm((DEPTH, d, N_EXPERTS), d ** -0.5),
        'moe_br': nrm((DEPTH, N_EXPERTS), 0.01),
        'moe_wgu': nrm((DEPTH, N_EXPERTS, d, 2 * EXPERT_FF), d ** -0.5),
        'moe_bgu': nrm((DEPTH, N_EXPERTS, 2 * EXPERT_FF), 0.01),
        'moe_wd': nrm((DEPTH, N_EXPERTS, EXPERT_FF, d), DN_BETA * EXPERT_FF ** -0.5),
        'moe_bd': nrm((DEPTH, N_EXPERTS, d), 0.01),
    }

def reference(x_prompt, x_sample, state_rwkv, state_rwkv_shift, cache_nsa_cmp, cache_nsa_slc,
              state_nsa_win, cache_dsa_kv, cache_dsa_idx, state_conv, page_table, c_prompt, c_sample,
              w_ada, b_ada, w_in, w_out, ln1_g, ln1_b, ln2_g, ln2_b,
              rwkv_mu, rwkv_w0, rwkv_w2, rwkv_a0, rwkv_a2, rwkv_g2, rwkv_kk, rwkv_ka, rwkv_rk,
              rwkv_gn_g, rwkv_gn_b, nsa_pe, nsa_w1, nsa_w2, conv_w,
              moe_wr, moe_br, moe_wgu, moe_bgu, moe_wd, moe_bd):
    slopes = _alibi_slopes(NSA_HEADS + DSA_HEADS)
    sl_nsa, sl_dsa = slopes[0::2], slopes[1::2]
    hp, hs = x_prompt, x_sample
    states_p, states_s = [], []
    for l in range(DEPTH):
        lp = {
            'w_ada': w_ada[l], 'b_ada': b_ada[l], 'w_in': w_in[l], 'w_out': w_out[l],
            'ln1_g': ln1_g[l], 'ln1_b': ln1_b[l], 'ln2_g': ln2_g[l], 'ln2_b': ln2_b[l],
            'rwkv_mu': rwkv_mu[l], 'rwkv_w0': rwkv_w0[l], 'rwkv_w2': rwkv_w2[l],
            'rwkv_a0': rwkv_a0[l], 'rwkv_a2': rwkv_a2[l], 'rwkv_g2': rwkv_g2[l],
            'rwkv_kk': rwkv_kk[l], 'rwkv_ka': rwkv_ka[l], 'rwkv_rk': rwkv_rk[l],
            'rwkv_gn_g': rwkv_gn_g[l], 'rwkv_gn_b': rwkv_gn_b[l],
            'nsa_pe': nsa_pe[l], 'nsa_w1': nsa_w1[l], 'nsa_w2': nsa_w2[l], 'conv_w': conv_w[l],
            'moe_wr': moe_wr[l], 'moe_br': moe_br[l], 'moe_wgu': moe_wgu[l], 'moe_bgu': moe_bgu[l],
            'moe_wd': moe_wd[l], 'moe_bd': moe_bd[l],
        }
        mix_p = functools.partial(_mixers_prompt, lp=lp, sl_nsa=sl_nsa, sl_dsa=sl_dsa)
        mix_s = functools.partial(
            _mixers_sample, lp=lp, sl_nsa=sl_nsa, sl_dsa=sl_dsa, s_rwkv=state_rwkv[l],
            s_shift=state_rwkv_shift[l], c_nsa_cmp=cache_nsa_cmp[l], c_nsa_slc=cache_nsa_slc[l],
            s_win=state_nsa_win[l], c_dsa_kv=cache_dsa_kv[l], c_dsa_idx=cache_dsa_idx[l],
            s_conv=state_conv[l], page_table=page_table)
        hp, st_p = _layer(hp, c_prompt, lp, mix_p)
        hs, st_s = _layer(hs, c_sample, lp, mix_s)
        states_p.append(st_p)
        states_s.append(st_s)
    rw_p, sh_p, ncmp_p, nslc_p, nwin_p, dkv_p, didx_p, conv_p = [jnp.stack(v) for v in zip(*states_p)]
    rw_s, sh_s, ncmp_s, nslc_s, nwin_s, dkv_s, didx_s, conv_s = [jnp.stack(v) for v in zip(*states_s)]
    return (hp, hs, rw_p, sh_p, ncmp_p, nslc_p, nwin_p, dkv_p, didx_p, conv_p,
            rw_s, sh_s, ncmp_s, nslc_s, nwin_s, dkv_s, didx_s, conv_s)


_drawn_inputs = setup_inputs


def setup_inputs(seed=0):
    import zlib

    import numpy as np

    out = dict(_drawn_inputs(seed))
    spreads = {}
    factors = {'cache_nsa_cmp': 2.685,
     'cache_nsa_slc': 4.424,
     'ln1_b': 2.697,
     'ln2_b': 2.952,
     'rwkv_kk': 16.323,
     'rwkv_rk': 3.814,
     'rwkv_gn_g': 28.75,
     'rwkv_gn_b': 58.4,
     'nsa_pe': 64.0,
     'moe_br': 22.739,
     'moe_bgu': 54.655,
     'moe_bd': 39.877}
    for name, (base, spread) in spreads.items():
        noise = np.random.default_rng([zlib.crc32(name.encode()), seed]).standard_normal(out[name].shape)
        drawn = base * np.exp(spread * noise) if base else spread * noise
        out[name] = jnp.asarray(drawn.astype(out[name].dtype))
    for name, factor in factors.items():
        out[name] = (out[name] * factor).astype(out[name].dtype)
    return out
```

```python
from contextlib import ExitStack

import numpy as np
import concourse.bass as bass
from concourse import mybir

F32 = mybir.dt.float32
I32 = mybir.dt.int32
U32 = mybir.dt.uint32
ALU = mybir.AluOpType
ACT = mybir.ActivationFunctionType
AX = mybir.AxisListType
ds = bass.ds

D = 1024
KD = D // 128
SEQ, DEC = 512, 8
NTOK = SEQ + DEC
HALF = NTOK // 2
NT = SEQ // 128
PAST, PAGE = 2048, 128
HD, GW, HEADS = 64, 256, 4
E, TOPK, FF = 32, 4, 1024
A_COLS, B_COLS, C_COLS = 896, 652, 548
IN_COLS = A_COLS + B_COLS + C_COLS + 768
B0, C0, D0 = A_COLS, A_COLS + B_COLS, A_COLS + B_COLS + C_COLS
DN_ALPHA = 2.0 ** 0.25
BIG = -1e30


class Chain:

    def __init__(self, sem):
        self.sem, self.n = sem, 0

    def __call__(self, eng, ins):
        self.n += 1
        ins.then_inc(self.sem, 1)
        eng.wait_ge(self.sem, self.n)


PIECES = [
    (0, 256, ["A0", "A1"]), (256, 256, ["A2", "A3"]), (512, 256, ["A4", "A5"]), (768, 128, ["A6"]),
    (B0, 256, ["N0", "N1"]), (B0 + 256, 256, ["V0", "V1"]), (B0 + 512, 140, ["V2", "GL"]),
    (C0, 256, ["D0", "D1"]), (C0 + 256, 256, ["V3", "QI"]), (C0 + 512, 36, ["KI"]),
    (D0, 256, ["Z0", "Z1"]), (D0 + 256, 256, ["Z2", "Z3"]), (D0 + 512, 256, ["Z4", "Z5"]),
]
RING_IN = 4


def build(nc, io):
    top = ExitStack()
    with top:
        def sem(name):
            return top.enter_context(nc.semaphore(name))

        def sbt(ctx, name, shape, dt=F32):
            return ctx.enter_context(nc.sbuf_tensor(name, shape, dt, side="right"))

        def keep(ctx, name, shape, dt=F32):
            return ctx.enter_context(nc.sbuf_tensor(name, shape, dt, side="left"))

        G = {}
        ps = top.enter_context(nc.psum_tensor("ps", [128, 8, 512], F32))
        G["ps"] = ps
        G["ident"] = keep(top, "ident", [128, 128])
        G["ones"] = keep(top, "ones", [128, 128])
        G["vlink"] = Chain(sem("vlink"))
        G["alink"] = Chain(sem("alink"))
        G["plink"] = Chain(sem("plink"))
        G["mod_dram"] = nc.dram_tensor("mod_dram", (9, 6 * D), F32, kind="Internal").ap()
        G["x2_dram"] = nc.dram_tensor("x2_dram", (NTOK, D), F32, kind="Internal").ap()
        G["outbuf"] = nc.dram_tensor("outbuf", ((MAX_CH + MAX_N) * SLOTS, D), F32, kind="Internal").ap()
        with ExitStack() as c:
            G["xh"] = sbt(c, "xh", [128, NT + 1, D])
            G["w_ring"] = sbt(c, "w_ring", [128, RING_IN, KD, 256])
            with ExitStack() as a:
                block_ada(nc, io, G, a, sem, sbt)
            G["mixT"] = keep(top, "mixT", [128, KD, NTOK])
            zctx = top.enter_context(ExitStack())
            G["zA"] = keep(zctx, "zA", [128, 7, NTOK])
            G["qN"] = keep(zctx, "qN", [64, HEADS, NTOK])
            G["qD"] = keep(zctx, "qD", [64, HEADS, NTOK])
            G["kvT"] = keep(zctx, "kvT", [128, 4, NTOK])
            G["qI"] = keep(zctx, "qI", [32, 4, NTOK])
            G["kI"] = keep(zctx, "kI", [36, NTOK])
            G["gl"] = keep(zctx, "gl", [12, NTOK])
            G["zD"] = keep(zctx, "zD", [128, 6, NTOK])
            with ExitStack() as b:
                block_proj(nc, io, G, b, sem, sbt)
        with ExitStack() as c:
            block_rwkv(nc, io, G, c, sem, sbt)
        G["rowsV"] = keep(zctx, "rowsV", [128, 4, NT, 128])
        G["kcT"] = keep(zctx, "kcT", [HD, NX - 1])
        G["vcR"] = keep(zctx, "vcR", [HD, 9, HD])
        G["gateR"] = keep(zctx, "gateR", [128, NT + 1, 12])
        G["wiR"] = keep(zctx, "wiR", [128, NT + 1, 4])
        G["blk_idx"] = keep(zctx, "blk_idx", [128, 4], I32)
        with ExitStack() as c:
            block_compress(nc, io, G, c, sem, sbt)
        with ExitStack() as c:
            attention_sems = []
            block_prompt_attention(nc, io, G, c, lambda name: attention_sems.append(nc.alloc_semaphore(name=name))
                                   or attention_sems[-1], sbt)
            nc.clear_and_free_semaphores(attention_sems)
            nc.all_engine_barrier()
        with ExitStack() as c:
            block_sample_attention(nc, io, G, c, sem, sbt)
        zctx.close()
        for name, shape, dt in (("slot_i", [128, NT + 1, TOPK], I32),
                                ("gateW", [128, NT + 1, TOPK], F32),
                                ("GT", [E, NTOK], F32),
                                ("tab", [1, 2, E + 1], I32),
                                ("rowtok", [SLOTS, MAX_CH + AHEAD], I32),
                                ("biasT", [128, E, 16], F32)):
            G[name] = keep(top, name, shape, dt)
        G["h2_dram"] = nc.dram_tensor("h2_dram", (NTOK, D), F32, kind="Internal").ap()
        with ExitStack() as c:
            block_out_router(nc, io, G, c, sem, sbt)
        with ExitStack() as c:
            block_experts(nc, io, G, c, sem, sbt)
        with ExitStack() as c:
            block_combine(nc, io, G, c, sem, sbt)


def block_ada(nc, io, G, ctx, sem, sbt):
    ps, ident, ones, xh, w_ring = G["ps"], G["ident"], G["ones"], G["xh"], G["w_ring"]
    vlink, alink, plink = G["vlink"], G["alink"], G["plink"]
    NP, W = 12, 512
    ring = sbt(ctx, "ada_ring", [128, 3, KD, W])
    crow = sbt(ctx, "crow", [9, D])
    cT = sbt(ctx, "cT", [128, KD, 9])
    mod = sbt(ctx, "mod", [9, 6 * D])
    st = sbt(ctx, "ln_st", [128, NT + 1, 2, 6])
    mv = sbt(ctx, "ln_mv", [128, NT + 1, 2])
    rstd = sbt(ctx, "ln_rstd", [128, NT + 1])
    x_in, c_in, b_in = sem("x_in"), sem("c_in"), sem("b_in")
    ada_in = [sem(f"ada_in{i}") for i in range(3)]
    G["w_in"] = w_in = [sem(f"w_in{i}") for i in range(RING_IN)]
    ident_ok, silu_ok, cT_mm, cT_ok = sem("ident_ok"), sem("silu_ok"), sem("cT_mm"), sem("cT_ok")
    ada_mm, ada_ev, mod_st = sem("ada_mm"), sem("ada_ev"), sem("mod_st")
    var_ok, rstd_ok = sem("var_ok"), sem("rstd_ok")

    with nc.Block() as block:
        @block.sync
        def _(sp):
            sp.dma_start(crow[0:1, :], io["c_prompt"]).then_inc(c_in, 16)
            sp.dma_start(crow[1:9, :], io["c_sample"]).then_inc(c_in, 16)
            for j in range(NP):
                if j >= 3:
                    sp.wait_ge(ada_mm, j - 2)
                sp.dma_start(ring[:, j % 3], io["w_ada"][0, :, j * W:(j + 1) * W]
                             .rearrange("(k p) n -> p k n", p=128)).then_inc(ada_in[j % 3], 16)
                if j == 2:
                    sp.dma_start(xh[:, 0:NT, :], io["x_prompt"][0].rearrange("(t p) d -> p t d", p=128))\
                        .then_inc(x_in, 16)
                    sp.dma_start(xh[0:DEC, NT, :], io["x_sample"].rearrange("b s d -> (b s) d")).then_inc(x_in, 16)
            for n in range(RING_IN):
                c0, w, _ = PIECES[n]
                sp.dma_start(w_ring[:, n, :, 0:w], io["w_in"][0, :, c0:c0 + w]
                             .rearrange("(k p) n -> p k n", p=128)).then_inc(w_in[n], 16)
            sp.wait_ge(ada_ev, NP)
            sp.dma_start(G["mod_dram"], mod[:]).then_inc(mod_st, 16)
            sp.wait_ge(mod_st, 16)

        @block.gpsimd
        def _(pool):
            plink(pool, nc.gpsimd.memset(ident[:], 0.0))
            nc.gpsimd.affine_select(out=ident[:], in_=ident[:], compare_op=ALU.not_equal, fill=1.0, base=0,
                                    pattern=[[-1, 128]], channel_multiplier=1).then_inc(ident_ok, 1)
            nc.gpsimd.memset(ones[:], 1.0).then_inc(ident_ok, 1)

        @block.scalar
        def _(act):
            act.dma_start(mod[:], bass.AP(io["b_ada"].tensor, 0, [[0, 9], [1, 6 * D]])).then_inc(b_in, 16)
            act.wait_ge(c_in, 32)
            act.activation(crow[:], crow[:], ACT.Silu).then_inc(silu_ok, 1)
            act.wait_ge(var_ok, 1)
            act.activation(rstd[:], rstd[:], ACT.Sqrt).then_inc(rstd_ok, 1)

        @block.tensor
        def _(pe):
            pe.wait_ge(ident_ok, 2)
            pe.wait_ge(silu_ok, 1)
            for k in range(KD):
                mm = pe.transpose(ps[:, 0, k * 9:k * 9 + 9], crow[:, k * 128:(k + 1) * 128], ident[0:9, 0:9])
            mm.then_inc(cT_mm, 1)
            pe.wait_ge(cT_ok, 1)
            for j in range(NP):
                pe.wait_ge(ada_in[j % 3], 16 * (j // 3 + 1))
                if j >= 2:
                    pe.wait_ge(ada_ev, j - 1)
                for k in range(KD):
                    mm = pe.matmul(ps[0:9, 1 + j % 2, :], cT[:, k, :], ring[:, j % 3, k, :],
                                   start=(k == 0), stop=(k == KD - 1))
                mm.then_inc(ada_mm, 1)

        @block.vector
        def _(v):
            v.wait_ge(cT_mm, 1)
            v.tensor_copy(cT[:].rearrange("p k n -> p (k n)"), ps[:, 0, 0:72]).then_inc(cT_ok, 1)
            v.wait_ge(x_in, 32)
            vlink(v, v.memset(mv[:], 1.0))
            for t in range(NT + 1):
                r = 128 if t < NT else DEC
                for i in range(2):
                    vlink(v, v.bn_stats(st[0:r, t, i], xh[0:r, t, i * 512:(i + 1) * 512]))
                vlink(v, v.bn_aggr(mv[0:r, t], st[0:r, t].rearrange("p a b -> p (a b)")))
            vlink(v, v.tensor_scalar(rstd[:], mv[:, :, 1], 1e-5, None, ALU.add))
            v.reciprocal(rstd[:], rstd[:]).then_inc(var_ok, 1)
            v.wait_ge(b_in, 16)

            def evacuate(j):
                v.wait_ge(ada_mm, j + 1)
                one = 1.0 if (j // 2) in (1, 4) else 0.0
                v.scalar_tensor_tensor(mod[:, j * W:(j + 1) * W], ps[0:9, 1 + j % 2, :], one,
                                       mod[:, j * W:(j + 1) * W], ALU.add, ALU.add).then_inc(ada_ev, 1)
            for j in range(3):
                evacuate(j)
            v.wait_ge(rstd_ok, 1)
            for t in range(NT + 1):
                r = 128 if t < NT else DEC
                v.tensor_scalar(xh[0:r, t, :], xh[0:r, t, :], mv[0:r, t, 0:1], rstd[0:r, t:t + 1],
                                ALU.subtract, ALU.mult)
                evacuate(3 + t)
            for j in range(NT + 4, NP):
                evacuate(j)


def block_proj(nc, io, G, ctx, sem, sbt):
    ps, ident, xh, w_ring, w_in = G["ps"], G["ident"], G["xh"], G["w_ring"], G["w_in"]
    vlink = G["vlink"]
    hT = sbt(ctx, "hT", [128, KD, NTOK])
    mod_p = sbt(ctx, "mod_p", [128, 2, D])
    mod_s = sbt(ctx, "mod_s", [DEC, 2, D])
    mod_in, h_ok, hT_mm, hT_ok = sem("mod_in"), sem("h_ok"), sem("hT_mm"), sem("hT_ok")
    z_mm, z_ev = sem("z_mm"), [sem("z_ev_v"), sem("z_ev_a")]
    chunks = [(n, i, c) for n, (_, _, cs) in enumerate(PIECES) for i, c in enumerate(cs)]
    last_chunk = {n: max(j for j, (m, _, _) in enumerate(chunks) if m == n) for n in range(len(PIECES))}

    def evac_parts(name):
        kind, i = name[0], name[1:]
        if kind == "A":
            return [(G["zA"][:, int(i), :], 0, 128, 1.0)]
        if kind == "Z":
            return [(G["zD"][:, int(i), :], 0, 128, 1.0)]
        if kind == "V":
            return [(G["kvT"][:, int(i), :], 0, 128, 1.0)]
        if kind in "ND":
            q = G["qN"] if kind == "N" else G["qD"]
            return [(q[:, 2 * int(i) + a, :], 64 * a, 64, HD ** -0.5) for a in range(2)]
        if name == "QI":
            return [(G["qI"][:, a, :], 32 * a, 32, 1.0) for a in range(4)]
        if name == "KI":
            return [(G["kI"][:, :], 0, 36, 1.0)]
        return [(G["gl"][:, :], 0, 12, 1.0)]

    with nc.Block() as block:
        @block.sync
        def _(sp):
            md = G["mod_dram"]
            sp.dma_start(mod_p[:], bass.AP(md.tensor, 0, [[0, 128], [D, 2], [1, D]])).then_inc(mod_in, 16)
            sp.dma_start(mod_s[:], md[1:9, 0:2 * D].rearrange("s (a d) -> s a d", a=2)).then_inc(mod_in, 16)
            for n in range(RING_IN, len(PIECES)):
                c0, w, _ = PIECES[n]
                sp.wait_ge(z_mm, last_chunk[n - RING_IN] + 1)
                sp.dma_start(w_ring[:, n % RING_IN, :, 0:w], io["w_in"][0, :, c0:c0 + w]
                             .rearrange("(k p) n -> p k n", p=128)).then_inc(w_in[n % RING_IN], 16)

        @block.vector
        def _(v):
            v.wait_ge(mod_in, 32)
            for t in [NT] + list(range(NT)):
                r, m = (128, mod_p) if t < NT else (DEC, mod_s)
                vlink(v, v.tensor_tensor(xh[0:r, t, :], xh[0:r, t, :], m[0:r, 1, :], ALU.mult))
                v.tensor_tensor(xh[0:r, t, :], xh[0:r, t, :], m[0:r, 0, :], ALU.add).then_inc(h_ok, 1)
            for j, (n, i, name) in enumerate(chunks):
                if j % 2:
                    continue
                v.wait_ge(z_mm, j + 1)
                b = 2 * (j % 4)
                parts = evac_parts(name)
                for dst, p0, rows, scale in parts:
                    ins = v.tensor_scalar(dst.rearrange("p (a n) -> p a n", a=2),
                                          ps[p0:p0 + rows, b:b + 2, 0:HALF], scale, None, ALU.mult)
                ins.then_inc(z_ev[0], 1)

        @block.scalar
        def _(act):
            for s, t in enumerate([NT] + list(range(NT))):
                r = 128 if t < NT else DEC
                act.wait_ge(hT_mm, s + 1)
                b = 2 * (s % 4)
                act.activation(hT[:, :, t * 128:t * 128 + r],
                               ps[:, b:b + 2, :].rearrange("p b (k t) -> p (b k) t", k=4)[:, :, 0:r],
                               ACT.Copy).then_inc(hT_ok, 1)
            for j, (n, i, name) in enumerate(chunks):
                if j % 2 == 0:
                    continue
                act.wait_ge(z_mm, j + 1)
                b = 2 * (j % 4)
                for dst, p0, rows, scale in evac_parts(name):
                    ins = act.activation(dst.rearrange("p (a n) -> p a n", a=2),
                                         ps[p0:p0 + rows, b:b + 2, 0:HALF], ACT.Copy, scale=scale)
                ins.then_inc(z_ev[1], 1)

        @block.tensor
        def _(pe):
            for s, t in enumerate([NT] + list(range(NT))):
                r = 128 if t < NT else DEC
                pe.wait_ge(h_ok, s + 1)
                if s >= 4:
                    pe.wait_ge(hT_ok, s - 3)
                b = 2 * (s % 4)
                for k in range(KD):
                    mm = pe.transpose(ps[:, b + k // 4, (k % 4) * 128:(k % 4) * 128 + r],
                                      xh[0:r, t, k * 128:(k + 1) * 128], ident[0:r, 0:r])
                mm.then_inc(hT_mm, 1)
            pe.wait_ge(hT_ok, NT + 1)
            for j, (n, i, name) in enumerate(chunks):
                if i == 0:
                    pe.wait_ge(w_in[n % RING_IN], 16 * (n // RING_IN + 1))
                if j >= 4:
                    pe.wait_ge(z_ev[j % 2], (j - 4) // 2 + 1)
                w = min(128, PIECES[n][1] - i * 128)
                b = 2 * (j % 4)
                for k in range(KD):
                    for a in range(2):
                        mm = pe.matmul(ps[0:w, b + a, 0:HALF], w_ring[:, n % RING_IN, k, i * 128:i * 128 + w],
                                       hT[:, k, a * HALF:(a + 1) * HALF], start=(k == 0), stop=(k == KD - 1))
                mm.then_inc(z_mm, 1)


CH = 64
NCH = SEQ // CH


def block_rwkv(nc, io, G, ctx, sem, sbt):
    ps, ident, ones = G["ps"], G["ident"], G["ones"]
    vlink, alink, plink = G["vlink"], G["alink"], G["plink"]
    zA, zD, mixT = G["zA"], G["zD"], G["mixT"]
    PRM = [("rwkv_mu", 7), ("rwkv_w0", 2), ("rwkv_a0", 2), ("rwkv_kk", 2), ("rwkv_ka", 2), ("rwkv_rk", 2),
           ("rwkv_gn_g", 2), ("rwkv_gn_b", 2), ("conv_w", 6)]
    first, at = {}, 0
    for name, n in PRM:
        first[name], at = at, at + n
    NPRM = at
    small = sbt(ctx, "small", [128, 128])
    prm = small[:, 0:NPRM]
    shT = small[:, 32:32 + 56].rearrange("p (c s) -> p c s", s=DEC)
    cvT = small[:, 96:128].rearrange("p (c s j) -> p c s j", c=2, j=2)
    par_buf = sbt(ctx, "par_buf", [128, 2, 12, HEADS, 128])
    pool_, used = par_buf[:].rearrange("p a b h t -> p (a b h t)"), [0]

    def early(rows_, n):
        used[0] += n
        return pool_[0:rows_, used[0] - n:used[0]]
    prow, shrow, cvrow = early(NPRM, 128), early(DEC, A_COLS), early(2 * DEC, GW)
    zrow, urow = early(9, A_COLS), early(DEC + 2, GW)
    lora = early(128, GW)
    notstart = early(128, SEQ)
    rep = early(128, 6 * HD).rearrange("p (x d) -> p x d", x=6)
    xexp = early(128, 6 * 2 * DEC * 4).rearrange("p (x c s q) -> p x c s q", x=6, c=2, q=4)

    def par(name, i):
        return prm[:, first[name] + i:first[name] + i + 1]

    vec = sbt(ctx, "vec", [128, 9, 2, NTOK])
    W, tmp, gg, kk, k2, bk, cum, kapW, nbW = (vec[:, i] for i in range(9))
    r, k, v_ = zA[:, 0:2], zA[:, 2:4], zA[:, 4:6]
    yT, bonus, scr = mixT[:, 0:2], mixT[:, 2:4], mixT[:, 4:6]
    u = mixT[:, 6:8]
    beta = scr
    reff = kapW
    rows = sbt(ctx, "rows", [128, 4, NT, GW])
    aR, vR, kR, bR = (rows[:, i] for i in range(4))
    xbuf = sbt(ctx, "xbuf", [128, 2, HEADS, HD])
    uR = sbt(ctx, "uR", [128, NT, GW])
    ST = sbt(ctx, "ST", [128, NCH + 1, 2, HD])
    MT = sbt(ctx, "MT", [128, NCH, 2, HD])
    NS = sbt(ctx, "NS", [128, NCH, 2, HD])
    masks = sbt(ctx, "masks", [128, 8, 128])
    mU, mUI, nUI, nU8, nL8, mB8, mB16, mB32 = (masks[:, i] for i in range(8))
    bones = sbt(ctx, "bones", [128, 128])
    stack64 = sbt(ctx, "stack64", [128, HD])
    vsel = sbt(ctx, "vsel", [128, 4])
    ssel = sbt(ctx, "ssel", [128, DEC])
    v16 = sbt(ctx, "v16", [128, 16])
    sk = sbt(ctx, "sk", [128, 16])
    y16 = sbt(ctx, "y16", [128, 16])
    vx = sbt(ctx, "vx", [128, 4, 16])
    sfin = sbt(ctx, "sfin", [HD, 2, 2, HD])

    p_in, s_in, m_ok = sem("p_in"), sem("s_in"), sem("m_ok")
    mm, ev = sem("rk_mm"), sem("rk_ev")
    tm = [sem("tile_mm0"), sem("tile_mm1")]
    tv = [sem("tile_ev0"), sem("tile_ev1")]
    lo_ok, act_ok, vec_ok = sem("lo_ok"), sem("act_ok"), sem("vec_ok")
    st_out = sem("st_out")
    row_ok = sem("row_ok")
    Sst = mixT[:, 2:6].rearrange("p c n -> p (c n)")
    S0 = Sst[:, 0:1024].rearrange("p (a b) -> p a b", a=16)
    S1 = Sst[:, 1024:2048].rearrange("p (a b) -> p a b", a=16)

    def halves(ap):
        return ap.rearrange("p (a n) -> p a n", a=2)

    def pair(b, rows_=slice(0, 128)):
        return ps[rows_, b:b + 2, 0:HALF]

    def heads4(m):
        return m.unsqueeze(1).broadcast_to((128, HEADS, 128))

    def bank4(b):
        return ps[:, b, :].rearrange("p (h t) -> p h t", h=HEADS)

    def pb(p, n):
        return par_buf[:, p, n]
    NtS, NS_, INt, IN2, N2, N2t, B8, B16, B32, HT, QT, PT = range(12)
    T_, Tt_, Y_, Pt_, IN4_, HV_ = NS_, NtS, N2, INt, IN2, N2t

    with nc.Block() as block:
        @block.sync
        def _(sp):
            for name, n in PRM:
                src = io[name]
                pat = {"conv_w": "a j (c p) -> (a j c) p", "rwkv_kk": "a (c h) d -> (a c) (h d)",
                       "rwkv_ka": "a (c h) d -> (a c) (h d)", "rwkv_rk": "a (c h) d -> (a c) (h d)"}
                if name in pat and name != "conv_w":
                    src = src.rearrange(pat[name], h=2)
                elif name == "conv_w":
                    src = src.rearrange(pat[name], p=128)
                else:
                    src = src.rearrange("a (c p) -> (a c) p", p=128)
                sp.dma_start(prow[first[name]:first[name] + n, :], src).then_inc(p_in, 16)
            sp.dma_start(shrow[:], io["state_rwkv_shift"][0]).then_inc(p_in, 16)
            sp.dma_start(cvrow[:], io["state_conv"][0].rearrange("s j c -> (s j) c")).then_inc(p_in, 16)
            sp.dma_start(lora[0:32, :], io["rwkv_w2"][0]).then_inc(p_in, 16)
            sp.dma_start(lora[32:64, :], io["rwkv_a2"][0]).then_inc(p_in, 16)
            sp.dma_start(lora[64:128, :], io["rwkv_g2"][0]).then_inc(p_in, 16)
            for h in range(HEADS):
                sp.dma_start(Sst[32 * h:32 * h + 32, 0:1024],
                             io["state_rwkv"][0, :, h].rearrange("s (q v) k -> s q (v k)", q=4)).then_inc(s_in, 16)
            sp.dma_start(io["out17"][0, :, 0, :], io["state_conv"][0, :, 1, :]).then_inc(st_out, 16)
            sp.wait_ge(row_ok, 1)
            sp.dma_start(io["out3"][0], zrow[0:1, :]).then_inc(st_out, 16)
            sp.dma_start(io["out11"][0], zrow[1:9, :]).then_inc(st_out, 16)
            sp.dma_start(io["out9"][0, 0], urow[0:2, :]).then_inc(st_out, 16)
            sp.dma_start(io["out17"][0, :, 1, :], urow[2:10, :]).then_inc(st_out, 16)
            sp.wait_ge(row_ok, 2)
            for h in range(HEADS):
                sp.dma_start(io["out10"][0, :, h].rearrange("s (q v) k -> s q (v k)", q=4),
                             Sst[32 * h:32 * h + 32, 0:1024]).then_inc(st_out, 16)
            sp.wait_ge(row_ok, 3)
            sp.dma_start(io["out2"][0, 0].rearrange("(c h) v k -> v c h k", h=2), sfin[:]).then_inc(st_out, 16)
            sp.wait_ge(st_out, 16 * 10)

        @block.gpsimd
        def _(pool):
            g = nc.gpsimd
            L = lambda i: plink(pool, i)

            def select(m, pattern, base, op, fill=0.0):
                sign = -1 if op in (ALU.is_lt, ALU.is_le) else 1
                op = {ALU.is_lt: ALU.is_gt, ALU.is_le: ALU.is_ge}.get(op, op)
                L(g.affine_select(out=m, in_=m, compare_op=op, fill=fill, base=sign * base,
                                  pattern=[[sign * a, n] for a, n in pattern], channel_multiplier=sign))

            def same_block(m, b):
                mv = m.rearrange("p (n b) -> p n b", b=b)
                select(mv, [[-b, 128 // b], [0, b]], 0, ALU.is_ge)
                select(mv, [[-b, 128 // b], [0, b]], -(b - 1), ALU.is_le)

            def fill(m, x):
                L(g.memset(m, x))
            for m, x, b, base, op in [(mU, 1.0, CH, 0, ALU.is_lt), (mUI, 1.0, CH, 0, ALU.is_le),
                                      (nUI, -1.0, CH, 0, ALU.is_le), (nU8, -1.0, 8, 0, ALU.is_lt),
                                      (nL8, -1.0, 8, 0, ALU.is_gt)]:
                fill(m, x)
                same_block(m, b)
                select(m, [[-1, 128]], base, op)
            for m, b in [(mB8, 8), (mB16, 16), (mB32, 32)]:
                fill(m, 0.0)
                mv = m.rearrange("p (n q b) -> p n q b", q=2, b=b)
                fill(mv[:, :, 1, :], 1.0)
                m3 = m.rearrange("p (n c) -> p n c", c=2 * b)
                select(m3, [[-2 * b, 64 // b], [0, 2 * b]], 0, ALU.is_ge)
                select(m3, [[-2 * b, 64 // b], [0, 2 * b]], -(b - 1), ALU.is_le)
            fill(bones[:], 1.0)
            same_block(bones[:], HD)
            fill(notstart[:], 1.0)
            fill(notstart[:].rearrange("p (c t) -> p c t", t=CH)[:, :, 0:1], 0.0)
            fill(ST[:, 0], 0.0)
            g.memset(sk[:], 0.0).then_inc(m_ok, 1)

        @block.scalar
        def _(act):
            A = lambda out, in_, f, **kw: alink(act, nc.scalar.activation(out, in_, f, **kw))
            act.wait_ge(lo_ok, 1)
            z6 = zA[:, 6, :]
            A(z6[0:32], z6[0:32], ACT.Tanh)
            nc.scalar.activation(z6[64:128], z6[64:128], ACT.Sigmoid).then_inc(act_ok, 1)
            act.wait_ge(mm, 2)
            for i in range(2):
                A(halves(W[:, i]), pair(2 * i), ACT.Sigmoid, bias=par("rwkv_w0", i))
                A(halves(tmp[:, i]), pair(4 + 2 * i), ACT.Sigmoid, bias=par("rwkv_a0", i))
            act.sem_inc(ev, 1)
            act.wait_ge(vec_ok, 1)
            nc.scalar.activation(cum, cum, ACT.Sqrt).then_inc(act_ok, 1)
            act.wait_ge(vec_ok, 2)
            A(tmp[:, :, 0:SEQ], tmp[:, :, 0:SEQ], ACT.Exp)
            nc.scalar.activation(W[:], W[:], ACT.Exp).then_inc(act_ok, 1)
            act.wait_ge(vec_ok, 3)
            nc.scalar.activation(tmp[:, :, 0:SEQ], cum[:, :, 0:SEQ], ACT.Exp, scale=-1.0).then_inc(act_ok, 1)
            act.wait_ge(vec_ok, 4)
            nc.scalar.activation(cum[:, :, 0:SEQ], cum[:, :, 0:SEQ], ACT.Exp).then_inc(act_ok, 1)

            def step(p, n, *copies):
                act.wait_ge(tm[p], n)
                for dst, src in copies:
                    nc.scalar.activation(dst, src, ACT.Copy).then_inc(tv[p], 1)
            for i0 in range(0, NT, 2):
                for n in range(14):
                    for p in range(2):
                        i, b, s = i0 + p, 4 * p, 14 * (i0 // 2) + n + 1
                        if n == 2:
                            step(p, s, (pb(p, N2t), bank4(b + 1)))
                        elif n == 3:
                            step(p, s, (pb(p, Pt_), bank4(b)))
                        elif n == 4:
                            step(p, s, (pb(p, Tt_), bank4(b + 1)))
                        elif n in (5, 7, 9):
                            step(p, s, (pb(p, Y_), bank4(b)))
                        elif n == 11:
                            step(p, s, (pb(p, HV_)[:, :, 0:HD], ps[:, b, 0:GW].rearrange("p (h d) -> p h d", h=HEADS)))
                        elif n == 12:
                            step(p, s, (uR[:, i, :], ps[:, b, 0:GW]))
            act.wait_ge(vec_ok, 5)
            nc.scalar.activation(scr, scr, ACT.Sqrt).then_inc(act_ok, 1)

        @block.tensor
        def _(pe):
            T = lambda out, in_, n: pe.transpose(out, in_, ident[0:n, 0:n])
            n_ev = [0]

            def done(ins):
                ins.then_inc(mm, 1)
                n_ev[0] += 1

            def ready():
                pe.wait_ge(ev, n_ev[0])
            pe.wait_ge(p_in, 16 * (len(PRM) + 5))
            T(ps[:, 0, 0:NPRM], prow[:], NPRM)
            for c in range(7):
                T(ps[:, 0, 32 + 8 * c:40 + 8 * c], shrow[:, c * 128:(c + 1) * 128], DEC)
            for c in range(2):
                T(ps[:, 0, 96 + 16 * c:112 + 16 * c], cvrow[:, c * 128:(c + 1) * 128], 2 * DEC)
            for c in range(7):
                m = pe.transpose(ps[0:9, 1 + c // 4, (c % 4) * 128:(c % 4) * 128 + 128], zA[:, c, SEQ - 1:NTOK], ident[:])
            done(m)
            pe.wait_ge(act_ok, 1)
            ready()
            for c in range(2):
                for b, p0, p1 in ((2 * c, 0, 32), (4 + 2 * c, 32, 64)):
                    for a in range(2):
                        m = pe.matmul(ps[:, b + a, 0:HALF], lora[p0:p1, c * 128:(c + 1) * 128],
                                      zA[p0:p1, 6, a * HALF:(a + 1) * HALF], start=True, stop=True)
            done(m)
            ready()
            for c in range(2):
                for a in range(2):
                    m = pe.matmul(ps[:, 2 * c + a, 0:HALF], lora[64:128, c * 128:(c + 1) * 128],
                                  zA[64:128, 6, a * HALF:(a + 1) * HALF], start=True, stop=True)
            pe.wait_ge(lo_ok, 2)
            for c in range(2):
                m = pe.transpose(ps[0:DEC + 2, 4, c * 128:(c + 1) * 128], u[:, c, SEQ - 2:NTOK], ident[:])
            done(m)
            pe.wait_ge(lo_ok, 3)
            pe.wait_ge(m_ok, 1)
            ready()

            def head_sums(src):
                for c in range(2):
                    for a in range(2):
                        m = pe.matmul(ps[:, 4 + 2 * c + a, 0:HALF], bones[:], src[:, c, a * HALF:(a + 1) * HALF],
                                      start=True, stop=True)
                return m
            done(head_sums(yT))
            pe.wait_ge(lo_ok, 4)
            ready()
            done(head_sums(yT))
            pe.wait_ge(lo_ok, 5)
            ready()
            for x in range(6):
                for h in range(HEADS):
                    hb = 64 * (h % 2)
                    m = pe.matmul(ps[32 * h:32 * h + 32, 0, x * HD:(x + 1) * HD],
                                  xexp[hb:hb + 64, x, h // 2].rearrange("p s q -> p (s q)"),
                                  ident[hb:hb + 64, hb:hb + 64], start=True, stop=True)
            done(m)
            pe.wait_ge(lo_ok, 6)
            ready()
            for h in range(HEADS):
                hb = 64 * (h % 2)
                m = pe.matmul(ps[hb:hb + 64, h // 2, 0:8],
                              vx[32 * h:32 * h + 32].rearrange("p q v -> p (q v)"),
                              ssel[32 * h:32 * h + 32, :], start=True, stop=True, tile_position=(32 * h, hb))
            done(m)
            pe.wait_ge(lo_ok, 7)
            ready()
            for x, src in enumerate((kk, v_, kapW, nbW)):
                for i in range(NT):
                    for c in range(2):
                        j = 2 * i + c
                        m = pe.transpose(ps[:, 2 * x + j // 4, (j % 4) * 128:(j % 4) * 128 + 128],
                                         src[:, c, i * 128:(i + 1) * 128], ident[:])
            done(m)
            ready()

            evs = [3, 5, 3, 2, 2, 1, 2, 1, 2, 1, 1, 2, 2, 1]
            seen = [0, 0]

            def four(out_bank, lhs, rhs, w=128):
                for h in range(HEADS):
                    m = pe.matmul(ps[:, out_bank, h * w:(h + 1) * w], lhs(h), rhs(h), start=True, stop=True)
                return m

            def gram(out_bank, o, lhs, rhs):
                for h in range(HEADS):
                    c = o + (h // 2) * 128
                    m = pe.matmul(ps[:, out_bank + h % 2, c:c + 128], lhs(h), rhs(h), start=True, stop=True)
                return m

            def t_layout(x, i):
                return lambda h: x[64 * (h % 2):64 * (h % 2) + 64, h // 2, i * 128:(i + 1) * 128]
            for i0 in range(0, NT, 2):
                for n in range(14):
                    for p in range(2):
                        i, b = i0 + p, 4 * p
                        if seen[p]:
                            pe.wait_ge(tv[p], seen[p])
                        B = lambda x: (lambda h: pb(p, x)[:, h, :])
                        al, rh, be, ka = t_layout(kk, i), t_layout(r, i), t_layout(beta, i), t_layout(k2, i)
                        R = lambda x: (lambda h: x[:, i, h * HD:(h + 1) * HD])
                        if n == 0:
                            gram(b, 0, ka, al)
                            gram(b, 256, be, rh)
                            m = gram(b + 2, 0, ka, rh)
                        elif n == 1:
                            gram(b, 0, be, al)
                            m = gram(b, 256, al, be)
                        elif n == 2:
                            four(b, B(NtS), B(NS_))
                            m = four(b + 1, B(NS_), B(NtS))
                        elif n == 3:
                            four(b, B(IN2), B(INt))
                            m = four(b + 1, B(N2t), B(N2))
                        elif n == 4:
                            four(b, B(Pt_), B(IN4_))
                            m = four(b + 1, B(IN4_), B(Pt_))
                        elif n in (5, 7, 9):
                            m = four(b, B((B8, B16, B32)[(n - 5) // 2]), B(T_))
                        elif n in (6, 8):
                            four(b, B(Tt_), B(Y_))
                            m = four(b + 1, B(Y_), B(Tt_))
                        elif n == 10:
                            m = four(b, B(Y_), B(Tt_))
                        elif n == 11:
                            four(b, B(HT), R(vR), HD)
                            m = four(b + 1, B(Tt_), R(aR), HD)
                        elif n == 12:
                            four(b, B(Tt_), lambda h: pb(p, HV_)[:, h, 0:HD], HD)
                            for h in range(HEADS):
                                hb = 64 * (h % 2)
                                pe.matmul(ps[hb:hb + 64, b + 1, (h // 2) * 128:(h // 2) * 128 + 128],
                                          xbuf[:, p, h], pb(p, QT)[:, h, :], start=True, stop=True)
                            for c2 in range(2):
                                for h in range(HEADS):
                                    hb, s = 64 * (h % 2), slice(64 * c2, 64 * c2 + 64)
                                    o = (h // 2) * HD
                                    m = pe.matmul(ps[hb:hb + 64, b + 2 + c2, o:o + HD], xbuf[s, p, h],
                                                  bR[s, i, h * HD:(h + 1) * HD], start=True, stop=True)
                        elif n == 13:
                            for h in range(HEADS):
                                hb, hs = 64 * (h % 2), slice(h * HD, (h + 1) * HD)
                                o = ps[hb:hb + 64, b, (h // 2) * 128:(h // 2) * 128 + 128]
                                pe.matmul(o, vR[:, i, hs], pb(p, PT)[:, h, :], start=True, stop=False)
                                m = pe.matmul(o, uR[:, i, hs], pb(p, QT)[:, h, :], start=False, stop=True)
                        m.then_inc(tm[p], 1)
                        seen[p] += evs[n]
            for p in range(2):
                pe.wait_ge(tv[p], seen[p])
            for c in range(NCH):
                for h in range(HEADS):
                    hb, s = 64 * (h % 2), slice(64 * (c % 2), 64 * (c % 2) + 64)
                    o = ps[hb:hb + 64, c % 2, (c // 2 * 2 + h // 2) * HD:(c // 2 * 2 + h // 2) * HD + HD]
                    hs = slice(h * HD, (h + 1) * HD)
                    pe.matmul(o, kR[s, c // 2, hs], vR[s, c // 2, hs], start=True, stop=False)
                    m = pe.matmul(o, bR[s, c // 2, hs], uR[s, c // 2, hs], start=False, stop=True)
            done(m)
            for c in range(NCH):
                ready()
                for h in range(HEADS):
                    hb = 64 * (h % 2)
                    m = pe.matmul(ps[hb:hb + 64, 2 + c % 2, (h // 2) * HD:(h // 2) * HD + HD],
                                  MT[hb:hb + 64, c, h // 2], ST[hb:hb + 64, c, h // 2], start=True, stop=True)
                done(m)
            ready()
            for i in range(NT):
                for h in range(HEADS):
                    hb, hs = 64 * (h % 2), slice(h * HD, (h + 1) * HD)
                    bank = 4 + 2 * (h // 2) + i // 2
                    o = ps[hb:hb + 64, bank, (i % 2) * 128:(i % 2) * 128 + 128]
                    for c2 in range(2):
                        pe.matmul(o[:, c2 * 64:c2 * 64 + 64], ST[hb:hb + 64, 2 * i + c2, h // 2],
                                  reff[hb:hb + 64, h // 2, i * 128 + c2 * 64:i * 128 + c2 * 64 + 64],
                                  start=True, stop=True)
            for c in range(2):
                m = pe.transpose(ps[0:HD, 0, c * 128:(c + 1) * 128], ST[:, NCH, c], ident[:])
            done(m)
            for n in (8, 9):
                pe.wait_ge(lo_ok, n)
                ready()
                done(head_sums((yT, scr)[n - 8]))

        @block.vector
        def _(v):
            L = lambda i: vlink(v, i)
            TT, TS, STT = v.tensor_tensor, v.tensor_scalar, v.scalar_tensor_tensor
            P_ = slice(0, SEQ)
            seen = [0]

            def step():
                seen[0] += 1
                v.wait_ge(mm, seen[0])
            L(v.tensor_reduce(vsel[:], ident[:].rearrange("p (a q) -> p q a", q=4), AX.X, ALU.add))
            idv = ident[:].rearrange("p (h s q) -> p s h q", h=4, q=4)
            L(v.tensor_reduce(ssel[:], idv, AX.XY, ALU.add))
            L(TT(stack64[:], ident[:, 0:HD], ident[:, HD:128], ALU.add))
            step()
            L(v.tensor_copy(small[:], ps[:, 0, 0:128]))
            L(v.tensor_copy(zrow[:, 0:512], ps[0:9, 1, :]))
            L(v.tensor_copy(zrow[:, 512:A_COLS], ps[0:9, 2, 0:384]))
            v.sem_inc(ev, 1)
            for c in (6, 0, 1, 2, 3, 4, 5):
                d = nbW[:, 0, :]
                L(TT(d[:, 1:SEQ], zA[:, c, 0:SEQ - 1], zA[:, c, 1:SEQ], ALU.subtract))
                L(TS(d[:, 0:1], zA[:, c, 0:1], -1.0, None, ALU.mult))
                L(TT(d[:, SEQ:NTOK], shT[:, c, :], zA[:, c, SEQ:NTOK], ALU.subtract))
                L(STT(zA[:, c, :], d, par("rwkv_mu", c), zA[:, c, :], ALU.mult, ALU.add))
                if c == 6:
                    v.sem_inc(lo_ok, 1)
            L(TT(u, zD[:, 2:4, :], zD[:, 4:6, :], ALU.mult))
            v.sem_inc(lo_ok, 1)
            for i in range(2):
                L(TS(kk[:, i], k[:, i], par("rwkv_kk", i), None, ALU.mult))
            L(TT(yT, kk, kk, ALU.mult))
            v.sem_inc(lo_ok, 1)
            step()
            step()
            for i in range(2):
                L(v.tensor_copy(halves(gg[:, i]), pair(2 * i)))
            L(v.tensor_copy(urow[:], ps[0:DEC + 2, 4, 0:GW]))
            v.sem_inc(row_ok, 1)
            v.sem_inc(ev, 1)
            for i in range(2):
                L(TS(k2[:, i], tmp[:, i], 1.0, par("rwkv_ka", i), ALU.subtract, ALU.mult))
            L(STT(k2, k2, 1.0, k, ALU.add, ALU.mult))
            step()
            for i in range(2):
                L(v.tensor_copy(halves(cum[:, i]), pair(4 + 2 * i)))
            v.sem_inc(ev, 1)
            v.sem_inc(vec_ok, 1)
            L(TT(yT, r, k2, ALU.mult))
            for i in range(2):
                L(TS(yT[:, i], yT[:, i], par("rwkv_rk", i), None, ALU.mult))
            v.sem_inc(lo_ok, 1)
            v.wait_ge(act_ok, 2)
            L(TS(cum, cum, 1e-12, None, ALU.max))
            L(v.reciprocal(cum, cum))
            L(TT(kk, kk, cum, ALU.mult))
            L(TT(bk, kk, tmp, ALU.mult))
            L(TS(W, W, -0.606531, None, ALU.mult))
            for i in range(2):
                L(v.tensor_tensor_scan(cum[:, i, P_], notstart[:], W[:, i, P_], 0.0, ALU.mult, ALU.add))
            L(TT(tmp[:, :, P_], cum[:, :, P_], W[:, :, P_], ALU.subtract))
            L(v.tensor_copy(W[:, :, P_], cum[:, :, P_]))
            v.sem_inc(vec_ok, 1)
            step()
            for i in range(2):
                L(TT(halves(nbW[:, i]), pair(4 + 2 * i), halves(v_[:, i]), ALU.mult))
            v.sem_inc(ev, 1)
            v.wait_ge(act_ok, 3)
            for x, src in enumerate((W, kk, bk, k2, r, v_)):
                L(v.tensor_copy(xexp[:, x], src[:, :, SEQ:NTOK].unsqueeze(3).broadcast_to((128, 2, DEC, 4))))
            v.sem_inc(lo_ok, 1)
            L(TT(kk[:, :, P_], kk[:, :, P_], tmp[:, :, P_], ALU.mult))
            v.sem_inc(vec_ok, 1)
            L(TT(r[:, :, P_], r[:, :, P_], W[:, :, P_], ALU.mult))
            step()
            L(v.tensor_copy(rep[:].rearrange("p x d -> p (x d)"), ps[:, 0, 0:6 * HD]))
            v.sem_inc(ev, 1)
            v.wait_ge(s_in, 64)

            def along_k(x):
                return rep[:, x].unsqueeze(1).broadcast_to((128, 16, HD))

            def along_v(x):
                return x.unsqueeze(2).broadcast_to((128, 16, HD))
            vselb = vsel[:].unsqueeze(2).broadcast_to((128, 4, 16))
            L(TT(vx[:], rep[:, 5].rearrange("p (q v) -> p q v", q=4), vselb, ALU.mult))
            L(v.tensor_reduce(v16[:], vx[:].rearrange("p q v -> p v q"), AX.X, ALU.add))
            L(TT(S1, S0, along_k(1), ALU.mult))
            L(v.tensor_reduce(sk[:], S1, AX.X, ALU.add))
            L(TT(S0, S0, along_k(0), ALU.mult))
            L(TT(S1, along_v(sk[:]), along_k(2), ALU.mult))
            L(TT(S0, S0, S1, ALU.subtract))
            L(TT(S1, along_v(v16[:]), along_k(3), ALU.mult))
            L(TT(S0, S0, S1, ALU.add))
            v.sem_inc(row_ok, 1)
            L(TT(S1, S0, along_k(4), ALU.mult))
            L(v.tensor_reduce(y16[:], S1, AX.X, ALU.add))
            L(TT(vx[:], y16[:].unsqueeze(1).broadcast_to((128, 4, 16)), vselb, ALU.mult))
            v.sem_inc(lo_ok, 1)
            step()
            L(v.tensor_copy(yT[:, :, SEQ:NTOK], ps[:, 0:2, 0:8]))
            v.sem_inc(ev, 1)
            v.wait_ge(st_out, 16 * 9)
            L(v.tensor_copy(bonus, nbW))
            v.wait_ge(act_ok, 4)
            L(TT(beta[:, :, P_], bk[:, :, P_], tmp[:, :, P_], ALU.mult))
            ce = cum[:, :, P_].rearrange("p c (n t) -> p c n t", t=CH)
            for i in range(2):
                last = ce[:, i, :, CH - 1:CH].broadcast_to((128, NCH, CH))
                L(TT(nbW[:, i, P_].rearrange("p (n t) -> p n t", t=CH), last, ce[:, i], ALU.subtract))
            L(v.tensor_copy(cum[:, :, P_], nbW[:, :, P_]))
            v.sem_inc(vec_ok, 1)
            v.wait_ge(act_ok, 5)
            L(STT(nbW[:, :, P_], bk[:, :, P_], -1.0, cum[:, :, P_], ALU.mult, ALU.mult))
            L(TT(kapW[:, :, P_], k2[:, :, P_], cum[:, :, P_], ALU.mult))
            L(TT(k2[:, :, P_], k2[:, :, P_], tmp[:, :, P_], ALU.mult))
            v.sem_inc(lo_ok, 1)
            step()
            for x, dst in enumerate((aR, vR, kR, bR)):
                L(v.tensor_copy(dst.rearrange("p t n -> p (t n)"), ps[:, 2 * x:2 * x + 2, :].rearrange("p a b -> p (a b)")))
            v.sem_inc(ev, 1)

            I4 = heads4(ident[:])

            def by_gram(x):
                return x.rearrange("p (c a) t -> p a c t", a=2)

            def gram4(b, o):
                return ps[:, b:b + 2, o:o + 256].rearrange("p a (c t) -> p a c t", c=2)

            def mask4(m):
                return m.unsqueeze(1).unsqueeze(1).broadcast_to((128, 2, 2, 128))
            for i0 in range(0, NT, 2):
                for n in range(14):
                    for p in range(2):
                        i, b = i0 + p, 4 * p
                        v.wait_ge(tm[p], 14 * (i0 // 2) + n + 1)

                        def put(ins, p=p):
                            ins.then_inc(tv[p], 1)
                        if n == 0:
                            put(TT(by_gram(pb(p, HT)), gram4(b, 0), mask4(mU), ALU.mult))
                            put(TT(by_gram(pb(p, QT)), gram4(b, 256), mask4(nUI), ALU.mult))
                            put(TT(by_gram(pb(p, PT)), gram4(b + 2, 0), mask4(mUI), ALU.mult))
                        elif n == 1:
                            L(TT(by_gram(pb(p, NtS)), gram4(b, 0), mask4(nU8), ALU.mult))
                            put(TT(pb(p, INt), pb(p, NtS), I4, ALU.add))
                            put(TT(by_gram(pb(p, B8)), gram4(b, 0), mask4(mB8), ALU.mult))
                            put(TT(by_gram(pb(p, B16)), gram4(b, 0), mask4(mB16), ALU.mult))
                            put(TT(by_gram(pb(p, B32)), gram4(b, 0), mask4(mB32), ALU.mult))
                            put(TT(by_gram(pb(p, NS_)), gram4(b, 256), mask4(nL8), ALU.mult))
                        elif n == 2:
                            put(TT(pb(p, IN2), bank4(b), I4, ALU.add))
                            put(v.tensor_copy(pb(p, N2), bank4(b)))
                        elif n == 3:
                            put(TT(pb(p, IN4_), bank4(b + 1), I4, ALU.add))
                        elif n == 4:
                            put(v.tensor_copy(pb(p, T_), bank4(b)))
                        elif n in (6, 8):
                            put(TT(pb(p, T_), pb(p, T_), bank4(b), ALU.subtract))
                            put(TT(pb(p, Tt_), pb(p, Tt_), bank4(b + 1), ALU.subtract))
                        elif n == 10:
                            put(TT(pb(p, Tt_), pb(p, Tt_), bank4(b), ALU.subtract))
                        elif n == 11:
                            put(v.tensor_copy(xbuf[:, p], ps[:, b + 1, 0:GW].rearrange("p (h d) -> p h d", h=HEADS)))
                        elif n == 12:
                            L(TT(reff[:, :, i * 128:(i + 1) * 128], ps[:, b + 1, 0:GW].rearrange("p (c t) -> p c t", c=2),
                                 r[:, :, i * 128:(i + 1) * 128], ALU.add))
                            for c2 in range(2):
                                for c in range(2):
                                    o = c * HD
                                    ch = 2 * i + c2
                                    L(STT(MT[:, ch, c], stack64[:], W[:, c, ch * CH + CH - 1:ch * CH + CH],
                                          ps[:, b + 2 + c2, o:o + HD], ALU.mult, ALU.add))
                            v.sem_inc(tv[p], 1)
                        elif n == 13:
                            put(v.tensor_copy(yT[:, :, i * 128:(i + 1) * 128],
                                              ps[:, b, 0:GW].rearrange("p (c t) -> p c t", c=2)))
            step()
            for a in range(2):
                L(v.tensor_copy(NS[:].rearrange("p (n a) h d -> p a n (h d)", a=2)[:, a],
                                ps[:, a, :].rearrange("p (n x) -> p n x", n=NCH // 2)))
            v.sem_inc(ev, 1)
            for c in range(NCH):
                step()
                TT(ST[:, c + 1], ps[:, 2 + c % 2, 0:128].rearrange("p (c d) -> p c d", c=2), NS[:, c], ALU.add).then_inc(ev, 1)
            step()
            L(v.tensor_copy(sfin[:].rearrange("p c h k -> p (c h k)"), ps[0:HD, 0, 0:GW]))
            v.sem_inc(row_ok, 1)
            for c in range(2):
                yc = yT[:, c, P_].rearrange("p (a t) -> p a t", a=2)
                L(TT(yc, ps[:, 4 + 2 * c:6 + 2 * c, 0:256], yc, ALU.add))
            v.sem_inc(ev, 1)
            v.sem_inc(lo_ok, 1)
            step()
            for c in range(2):
                L(STT(halves(yT[:, c]), pair(4 + 2 * c), -1.0 / HD, halves(yT[:, c]), ALU.mult, ALU.add))
            L(TT(scr, yT, yT, ALU.mult))
            v.sem_inc(ev, 1)
            v.sem_inc(lo_ok, 1)
            step()
            for c in range(2):
                L(TS(halves(scr[:, c]), pair(4 + 2 * c), 1.0 / HD, 64e-5, ALU.mult, ALU.add))
            L(v.reciprocal(scr, scr))
            v.sem_inc(vec_ok, 1)
            for c in range(2):
                w0, w1, w2 = (par("conv_w", 2 * j + c) for j in range(3))
                y, uc, cv = cum[:, c], u[:, c], cvT[:, c]
                L(TS(y, uc, w2, None, ALU.mult))
                L(STT(y[:, 1:SEQ], uc[:, 0:SEQ - 1], w1, y[:, 1:SEQ], ALU.mult, ALU.add))
                L(STT(y[:, 2:SEQ], uc[:, 0:SEQ - 2], w0, y[:, 2:SEQ], ALU.mult, ALU.add))
                L(STT(y[:, SEQ:], cv[:, :, 1], w1, y[:, SEQ:], ALU.mult, ALU.add))
                L(STT(y[:, SEQ:], cv[:, :, 0], w0, y[:, SEQ:], ALU.mult, ALU.add))
            L(TT(u, cum, zD[:, 0:2, :], ALU.mult))
            v.wait_ge(act_ok, 6)
            L(TT(yT, yT, scr, ALU.mult))
            for c in range(2):
                L(TS(yT[:, c], yT[:, c], par("rwkv_gn_g", c), par("rwkv_gn_b", c), ALU.mult, ALU.add))
            L(TT(yT, yT, bonus, ALU.add))
            L(TT(yT, yT, gg, ALU.mult))


NB_DEC = PAST // 32
NB_P = SEQ // 32
NBLK = DEC * NB_DEC
NX = NBLK + NB_P + 1


def block_compress(nc, io, G, ctx, sem, sbt):
    ps, ident = G["ps"], G["ident"]
    vlink, alink, plink = G["vlink"], G["alink"], G["plink"]
    kvT, kI, gl, rowsV, kcT, vcR, gateR, wiR = (G[n] for n in ("kvT", "kI", "gl", "rowsV", "kcT", "vcR", "gateR", "wiR"))
    blk = sbt(ctx, "blk", [128, 5, 4096])
    w1 = sbt(ctx, "w1", [128, 2, 16, 128])
    w2 = sbt(ctx, "w2", [128, 2, HD])
    pt4 = sbt(ctx, "pt4", [128, 4], I32)
    idx = G["blk_idx"]
    sub = sbt(ctx, "sub", [128, 1], F32)
    ptf = sbt(ctx, "ptf", [128, 4], F32)
    sq = sbt(ctx, "sq", [128, 4, 32], F32)
    xT = sbt(ctx, "xT", [128, 2, 2, NBLK])
    xX = sbt(ctx, "xX", [128, 2, 16, NX - NBLK])
    hid = sbt(ctx, "hid", [128, 2, NX - 1])
    pebias = sbt(ctx, "pebias", [128, 2])
    kiR = sbt(ctx, "kiR", [128, NT + 1, 36])
    glR = sbt(ctx, "glR", [128, NT + 1, 12])
    dec4 = sbt(ctx, "dec4", [DEC, 4, 128])
    w_in_, pt_in, idx_ok, blk_in, cmp_st, row_out = (sem(n) for n in ("cw_in", "pt_in", "idx_ok", "blk_in", "cmp_st", "row_out"))
    r_mm, r_ev, t_mm, h_mm, g_ok, o_mm = (sem(n) for n in ("r_mm", "r_ev", "ct_mm", "ch_mm", "cg_ok", "co_mm"))
    tv_ev, ta_ev, x_ev = sem("ct_ev_v"), sem("ct_ev_a"), sem("cx_ev")
    OUTS = (4, 5, 6, 7)

    with nc.Block() as block:
        @block.sync
        def _(sp):
            for t in range(4):
                sp.dma_start(pt4[:, t:t + 1], bass.AP(io["page_table"].tensor, 32 * t, [[1, 32], [0, 4], [1, 1]]))\
                    .then_inc(pt_in, 16)
            sp.dma_start(w1[:], io["nsa_w1"][0].rearrange("c (j p) h -> p c j h", p=128)).then_inc(w_in_, 16)
            sp.dma_start(w2[:], io["nsa_w2"][0].rearrange("c h d -> h c d")).then_inc(w_in_, 16)
            sp.dma_start(blk[16:17, 4, :], io["nsa_pe"].rearrange("a j c d -> a (j c d)")).then_inc(w_in_, 16)
            n = 0
            sp.dma_start(io["out14"][0, :, 0:511], io["state_nsa_win"][0, :, 1:512]).then_inc(row_out, 16)
            n += 1
            for c in range(4):
                sp.wait_ge(r_ev, c + 1)
                s = cmp_st if c == 0 else row_out
                n += c != 0
                sp.dma_start(io[f"out{OUTS[c]}"][0, 0].rearrange("(t p) a d -> p t (a d)", p=128),
                             rowsV[:, c]).then_inc(s, 16)
            sp.wait_ge(cmp_st, 16)
            sp.dma_start(blk[0:NB_P, 4, :], io["out4"][0, 0].rearrange("(n j) a d -> n (j a d)", n=NB_P))\
                .then_inc(w_in_, 16)
            sp.wait_ge(r_ev, 5)
            for c, o in ((0, 12), (1, 13), (3, 15)):
                sp.dma_start(io[f"out{o}"][0].rearrange("s b a d -> s (b a d)"), dec4[:, c]).then_inc(row_out, 16)
            sp.dma_start(io["out14"][0, :, 511].rearrange("s a d -> s (a d)"), dec4[:, 2]).then_inc(row_out, 16)
            sp.dma_start(io["out8"][0, 0].rearrange("(t p) d -> p t d", p=128), kiR[:, 0:NT, 0:32]).then_inc(row_out, 16)
            sp.dma_start(io["out16"][0, :, 0], kiR[0:DEC, NT, 0:32]).then_inc(row_out, 16)
            sp.wait_ge(row_out, 16 * (n + 6))

        @block.gpsimd
        def _(pool):
            g = nc.gpsimd
            pool.wait_ge(idx_ok, 1)
            for t in range(4):
                g.indirect_dma_start(blk[:, t, :], None, io["cache_nsa_cmp"][0].rearrange("n (s j) a d -> (n s) (j a d)", s=4),
                                     bass.IndirectOffsetOnAxis(ap=idx[:, t:t + 1], axis=0)).then_inc(blk_in, 16)

        @block.vector
        def _(v):
            L = lambda i: vlink(v, i)
            L(v.tensor_reduce(sq[:, 0, 0:4], ident[:].rearrange("p (a q) -> p q a", q=4), AX.X, ALU.add))
            L(v.scalar_tensor_tensor(sub[:], sq[:, 0, 3:4], 1.5, sq[:, 0, 2:3], ALU.mult, ALU.add))
            L(v.scalar_tensor_tensor(sub[:], sub[:], 2.0, sq[:, 0, 1:2], ALU.mult, ALU.add))
            v.wait_ge(pt_in, 64)
            L(v.tensor_copy(ptf[:], pt4[:]))
            L(v.tensor_scalar(ptf[:], ptf[:], 4.0, sub[:], ALU.mult, ALU.add))
            L(v.tensor_copy(idx[:], ptf[:]))
            v.sem_inc(idx_ok, 1)
            for c in range(4):
                v.wait_ge(r_mm, c + 1)
                v.tensor_copy(rowsV[:, c].rearrange("p t n -> p (t n)"), ps[:, c % 4, :]).then_inc(r_ev, 1)
            v.wait_ge(r_mm, 5)
            L(v.tensor_copy(dec4[:].rearrange("p c n -> p (c n)"), ps[0:DEC, 4, :]))
            L(v.tensor_copy(kiR[:, 0:NT].rearrange("p t n -> p (t n)"), ps[:, 5, 0:144]))
            L(v.tensor_copy(kiR[0:DEC, NT], ps[0:DEC, 5, 144:180]))
            L(v.tensor_copy(glR[:, 0:NT].rearrange("p t n -> p (t n)"), ps[:, 5, 192:240]))
            L(v.tensor_copy(glR[0:DEC, NT], ps[0:DEC, 5, 240:252]))
            L(v.tensor_copy(wiR[:, 0:NT], kiR[:, 0:NT, 32:36]))
            L(v.tensor_copy(wiR[0:DEC, NT], kiR[0:DEC, NT, 32:36]))
            v.sem_inc(r_ev, 1)
            v.wait_ge(t_mm, 1)
            for c in range(2):
                for q in range(2):
                    L(v.tensor_copy(xX[64 * q:64 * q + 64, c].rearrange("p j n -> p (j n)"),
                                    ps[64 * c:64 * c + 64, q, 0:16 * (NX - NBLK)]))
            v.sem_inc(x_ev, 1)
            for n in range(16):
                v.wait_ge(t_mm, n + 2)
                if n >= 2:
                    v.wait_ge(h_mm, n)
                b = 2 * (n % 2)
                v.tensor_copy(xT[0:64, n % 2, 0], ps[0:64, b, :]).then_inc(tv_ev, 1)
                v.tensor_copy(xT[64:128, n % 2, 1], ps[64:128, b + 1, :]).then_inc(tv_ev, 1)
            v.wait_ge(h_mm, 1)
            for c in range(2):
                L(v.tensor_copy(pebias[:, c:c + 1], ps[:, 6 + c, NB_P:NB_P + 1]))
            v.sem_inc(g_ok, 1)
            v.wait_ge(o_mm, 1)
            L(v.tensor_copy(kcT[:, 0:NBLK], ps[0:HD, 0, :]))
            L(v.tensor_copy(kcT[:, NBLK:NX - 1], ps[0:HD, 1, 0:NB_P]))
            L(v.tensor_copy(vcR[:, 0:8].rearrange("p s d -> p (s d)"), ps[0:HD, 2, :]))
            L(v.tensor_copy(vcR[0:NB_P, 8], ps[0:NB_P, 3, 0:HD]))

        @block.scalar
        def _(act):
            for n in range(16):
                act.wait_ge(t_mm, n + 2)
                if n >= 2:
                    act.wait_ge(h_mm, n)
                b = 2 * (n % 2)
                nc.scalar.activation(xT[0:64, n % 2, 1], ps[64:128, b, :], ACT.Copy).then_inc(ta_ev, 1)
                nc.scalar.activation(xT[64:128, n % 2, 0], ps[0:64, b + 1, :], ACT.Copy).then_inc(ta_ev, 1)
            act.wait_ge(h_mm, 17)
            act.wait_ge(g_ok, 1)
            for c in range(2):
                alink(act, nc.scalar.activation(hid[:, c, 0:NBLK], ps[:, 4 + c, :],
                                                ACT.Gelu_apprx_tanh, bias=pebias[:, c:c + 1]))
                alink(act, nc.scalar.activation(hid[:, c, NBLK:NX - 1], ps[:, 6 + c, 0:NB_P],
                                                ACT.Gelu_apprx_tanh, bias=pebias[:, c:c + 1]))
            act.sem_inc(g_ok, 1)
            act.wait_ge(r_ev, 5)
            alink(act, nc.scalar.activation(gateR[:, 0:NT], glR[:, 0:NT], ACT.Sigmoid))
            alink(act, nc.scalar.activation(gateR[0:DEC, NT], glR[0:DEC, NT], ACT.Sigmoid))

        @block.tensor
        def _(pe):
            for c in range(4):
                for t in range(NT):
                    m = pe.transpose(ps[:, c, t * 128:(t + 1) * 128], kvT[:, c, t * 128:(t + 1) * 128], ident[:])
                m.then_inc(r_mm, 1)
            for c in range(4):
                pe.transpose(ps[0:DEC, 4, c * 128:(c + 1) * 128], kvT[:, c, SEQ:NTOK], ident[:])
            for t in range(NT + 1):
                w = 128 if t < NT else DEC
                pe.transpose(ps[0:w, 5, t * 36:(t + 1) * 36], kI[:, t * 128:t * 128 + w], ident[0:36, 0:36])
            for t in range(NT + 1):
                w = 128 if t < NT else DEC
                m = pe.transpose(ps[0:w, 5, 192 + t * 12:204 + t * 12], gl[:, t * 128:t * 128 + w], ident[0:12, 0:12])
            m.then_inc(r_mm, 1)
            pe.wait_ge(r_ev, 5)
            pe.wait_ge(w_in_, 64)

            xr = NX - NBLK
            for j in range(32):
                m = pe.transpose(ps[:, j % 2, (j // 2) * xr:(j // 2 + 1) * xr], blk[0:xr, 4, j * 128:(j + 1) * 128],
                                 ident[0:xr, 0:xr])
            m.then_inc(t_mm, 1)
            pe.wait_ge(x_ev, 1)
            for c in range(2):
                for j in range(16):
                    m = pe.matmul(ps[:, 6 + c, 0:xr], w1[:, c, j, :], xX[:, c, j, :], start=(j == 0), stop=(j == 15))
            m.then_inc(h_mm, 1)
            pe.wait_ge(blk_in, 64)

            def turn(n):
                if n >= 2:
                    pe.wait_ge(tv_ev, 2 * (n - 1))
                    pe.wait_ge(ta_ev, 2 * (n - 1))
                for q in range(2):
                    for t in range(4):
                        j = 2 * n + q
                        m = pe.transpose(ps[:, 2 * (n % 2) + q, t * 128:(t + 1) * 128],
                                         blk[:, t, j * 128:(j + 1) * 128], ident[:])
                m.then_inc(t_mm, 1)

            turn(0)
            for n in range(16):
                if n + 1 < 16:
                    turn(n + 1)
                pe.wait_ge(tv_ev, 2 * (n + 1))
                pe.wait_ge(ta_ev, 2 * (n + 1))
                for c in range(2):
                    m = pe.matmul(ps[:, 4 + c, :], w1[:, c, n, :], xT[:, n % 2, c], start=(n == 0), stop=(n == 15))
                m.then_inc(h_mm, 1)
            pe.wait_ge(g_ok, 2)
            pe.matmul(ps[0:HD, 0, :], w2[:, 0, :], hid[:, 0, 0:NBLK], start=True, stop=True)
            pe.matmul(ps[0:HD, 1, 0:NB_P], w2[:, 0, :], hid[:, 0, NBLK:NX - 1], start=True, stop=True)
            for s in range(DEC):
                pe.matmul(ps[0:HD, 2, s * HD:(s + 1) * HD], hid[:, 1, s * NB_DEC:(s + 1) * NB_DEC], w2[:, 1, :],
                          start=True, stop=True)
            pe.matmul(ps[0:NB_P, 3, 0:HD], hid[:, 1, NBLK:NX - 1], w2[:, 1, :], start=True, stop=True).then_inc(o_mm, 1)


SLOPES = [2.0 ** -(i + 1) for i in range(8)]
K_SEL = 128
SLC, WIN, DSA = 1, 2, 3
assert SEQ // 64 <= 16 and SEQ <= 512


def block_prompt_attention(nc, io, G, ctx, sem, sbt):
    ps, ident = G["ps"], G["ident"]
    vlink, alink, plink = G["vlink"], G["alink"], G["plink"]
    kvT, kI, qI, qN, qD, mixT = (G[n] for n in ("kvT", "kI", "qI", "qN", "qD", "mixT"))
    rowsV, kcT, vcR, gateR, wiR = (G[n] for n in ("rowsV", "kcT", "vcR", "gateR", "wiR"))
    disti = sbt(ctx, "disti", [128, 512], I32)
    dist = sbt(ctx, "dist", [128, 512])
    ali = sbt(ctx, "ali", [128, 8, 512])
    cdist = sbt(ctx, "cdist", [128, NT, NB_P])
    cbias = sbt(ctx, "cbias", [128, NT, HEADS, NB_P])
    score = sbt(ctx, "score", [128, 512])
    rel = sbt(ctx, "rel", [128, 2, 512])
    selb = sbt(ctx, "selb", [128, HEADS, 512])
    top8 = sbt(ctx, "top8", [128, 8])
    P = sbt(ctx, "P", [128, 3, 512])
    PT = sbt(ctx, "PTt", [128, 2, 512])
    pc = sbt(ctx, "pc", [128, HEADS, NB_P])
    pcT = sbt(ctx, "pcT", [NB_P, HEADS, 128])
    mx = sbt(ctx, "mx", [128, 3])
    sm = sbt(ctx, "sm", [128, 3])
    rc = sbt(ctx, "rc", [128, 3])
    cm = sbt(ctx, "cm", [128, 4])
    cs = sbt(ctx, "cs", [128, 4])
    cst_ok = sem("at_cst")
    c_mm, c_v, c_a, c_pT, e_c = sem("c_mm"), sem("c_v"), sem("c_a"), sem("c_pT"), sem("e_c")
    i_mm, i_rel, i_use, sc_ok, sc_done, sel_ok, selb_ok, dsa_free = (sem("at_" + n) for n in (
        "i_mm", "i_rel", "i_use", "sc_ok", "sc_done", "sel_ok", "selb_ok", "dsa_free"))
    s_mm, s_ok, e_ok, p_ok, t_mm, t_ok, o_mm, o_ok = (sem("at_" + n) for n in (
        "s_mm", "s_ok", "e_ok", "p_ok", "t_mm", "t_ok", "o_mm", "o_ok"))
    units = [(i, h, b) for i in range(NT) for g in (0, 1) for h in range(HEADS)
             for b in ((SLC, WIN) if g == 0 else (DSA,))]
    PER = len(units) // NT
    N = len(units)
    ROUNDS = K_SEL // 8

    def nk(i):
        return (i + 1) * 128

    def group(u):
        i, h, b = units[u]
        return (8 * i + h, b == SLC, b == WIN) if b != DSA else (8 * i + 4 + h, True, True)

    zero = sbt(ctx, "zero", [128, D])
    zero_ok, zero_st = sem("at_zero_ok"), sem("at_zero_st")

    with nc.Block() as block:
        @block.sync
        def _(sp):
            sp.wait_ge(zero_ok, 1)
            for g in range(E, MAX_CH + 1):
                sp.dma_start(G["outbuf"][g * SLOTS:(g + 1) * SLOTS], zero[:]).then_inc(zero_st, 16)
            sp.wait_ge(zero_st, 16 * (MAX_CH + 1 - E))

        @block.gpsimd
        def _(pool):
            g = nc.gpsimd
            L = lambda i: plink(pool, i)
            g.memset(zero[:], 0.0).then_inc(zero_ok, 1)
            L(g.iota(disti[:], pattern=[[-1, 512]], base=384, channel_multiplier=1))
            L(g.tensor_copy(dist[:], disti[:]))
            for s in range(8):
                L(g.tensor_scalar(ali[:, s], dist[:], -SLOPES[s], None, ALU.mult))
                L(g.affine_select(out=ali[:, s], in_=ali[:, s], compare_op=ALU.is_ge, fill=BIG, base=384,
                                  pattern=[[-1, 512]], channel_multiplier=1))
            L(g.iota(disti[:, 0:NT * NB_P].rearrange("p (t n) -> p t n", t=NT), pattern=[[128, NT], [-32, NB_P]],
                     base=-31, channel_multiplier=1))
            L(g.tensor_copy(cdist[:].rearrange("p t n -> p (t n)"), disti[:, 0:NT * NB_P]))
            for h in range(HEADS):
                L(g.tensor_scalar(cbias[:, :, h], cdist[:], -SLOPES[2 * h], None, ALU.mult))
                L(g.affine_select(out=cbias[:, :, h], in_=cbias[:, :, h], compare_op=ALU.is_ge, fill=BIG, base=-31,
                                  pattern=[[128, NT], [-32, NB_P]], channel_multiplier=1))
            pool.sem_inc(cst_ok, 1)
            for i in range(NT):
                pool.wait_ge(sc_ok, i + 1)
                L(g.affine_select(out=score[:, 0:nk(i)], in_=score[:, 0:nk(i)], compare_op=ALU.is_ge, fill=BIG,
                                  base=128 * i, pattern=[[-1, nk(i)]], channel_multiplier=1))
                pool.sem_inc(sc_done, 1)
                pool.wait_ge(sel_ok, i + 1)
                if i >= 1:
                    pool.wait_ge(s_ok, PER * i)
                for h in range(HEADS):
                    L(g.tensor_tensor(selb[:, h, 0:nk(i)], score[:, 0:nk(i)], ali[:, 2 * h + 1, 512 - nk(i):512], ALU.add))
                pool.sem_inc(selb_ok, 1)

        @block.tensor
        def _(pe):
            def tile_start(i):
                q = slice(i * 128, (i + 1) * 128)
                for h in range(HEADS):
                    m = pe.matmul(ps[:, 6, h * NB_P:(h + 1) * NB_P], qN[:, h, q], kcT[:, NBLK:NBLK + NB_P],
                                  start=True, stop=True)
                m.then_inc(c_mm, 1)
                pe.wait_ge(c_v, i + 1)
                for h in range(HEADS):
                    m = pe.transpose(ps[0:NB_P, 7, h * 128:(h + 1) * 128], pc[:, h, :], ident[:])
                m.then_inc(c_mm, 1)
                pe.wait_ge(c_pT, i + 1)
                for h in range(HEADS):
                    n = 4 * i + h
                    if h >= 2:
                        pe.wait_ge(i_rel, n - 1)
                    pe.matmul(ps[:, 6 + h % 2, 0:nk(i)], qI[:, h, q], kI[0:32, 0:nk(i)], start=True, stop=True)\
                        .then_inc(i_mm, 1)

            def scores(u):
                i, h, b = units[u]
                if u >= 2:
                    pe.wait_ge(s_ok, u - 1)
                q = (qD if b == DSA else qN)[:, h, i * 128:(i + 1) * 128]
                pe.matmul(ps[:, u % 2, 0:nk(i)], q, kvT[0:HD, b, 0:nk(i)], start=True, stop=True).then_inc(s_mm, 1)

            def turn(u):
                i = units[u][0]
                pe.wait_ge(p_ok, u + 1)
                if u >= 2:
                    pe.wait_ge(t_ok, u - 1)
                for k in range(i + 1):
                    m = pe.transpose(ps[:, 2 + u % 2, k * 128:(k + 1) * 128], P[:, u % 3, k * 128:(k + 1) * 128], ident[:])
                m.then_inc(t_mm, 1)

            def output(u):
                i, h, b = units[u]
                g, first, last = group(u)
                hb = 64 * (h % 2)
                o = ps[hb:hb + 64, 4 + g % 2, 0:128]
                pe.wait_ge(t_ok, u + 1)
                if first and g >= 2:
                    pe.wait_ge(o_ok, g - 1)
                if b == SLC:
                    pe.matmul(o, vcR[0:NB_P, 8, :], pcT[:, h, :], start=True, stop=False)
                for k in range(i + 1):
                    m = pe.matmul(o, rowsV[:, b, k, HD:128], PT[:, u % 2, k * 128:(k + 1) * 128],
                                  start=(k == 0 and b == DSA), stop=(last and k == i))
                m.then_inc(o_mm, 1)

            pe.wait_ge(cst_ok, 1)
            scores(0)
            for u in range(N + 2):
                if u < N and u % PER == 0:
                    tile_start(u // PER)
                if u + 1 < N:
                    scores(u + 1)
                if 1 <= u <= N:
                    turn(u - 1)
                if u >= 2:
                    output(u - 2)

        @block.scalar
        def _(act):
            for u in range(N + 1):
                if u < N and u % PER == 0:
                    i = u // PER
                    act.wait_ge(c_a, i + 1)
                    nc.scalar.activation(pc[:], pc[:], ACT.Exp).then_inc(e_c, 1)
                    act.wait_ge(c_mm, 2 * (i + 1))
                    if i >= 1:
                        act.wait_ge(o_mm, PER * (i - 1) + 7)
                    nc.scalar.activation(pcT[:].rearrange("p h t -> p (h t)"), ps[0:NB_P, 7, :], ACT.Copy).then_inc(c_pT, 1)
                    for h in range(HEADS):
                        n = 4 * i + h
                        act.wait_ge(i_mm, n + 1)
                        if n >= 2:
                            act.wait_ge(i_use, n - 1)
                        nc.scalar.activation(rel[:, n % 2, 0:nk(i)], ps[:, 6 + h % 2, 0:nk(i)], ACT.Relu).then_inc(i_rel, 1)
                if u < N:
                    i = units[u][0]
                    act.wait_ge(s_ok, u + 1)
                    nc.scalar.activation(P[:, u % 3, 0:nk(i)], P[:, u % 3, 0:nk(i)], ACT.Exp, bias=mx[:, u % 3:u % 3 + 1],
                                         accum_out=sm[:, u % 3:u % 3 + 1]).then_inc(e_ok, 1)
                if u >= 1:
                    i = units[u - 1][0]
                    act.wait_ge(t_mm, u)
                    if u >= 3:
                        act.wait_ge(o_mm, u - 2)
                    nc.scalar.activation(PT[:, (u - 1) % 2, 0:nk(i)], ps[:, 2 + (u - 1) % 2, 0:nk(i)], ACT.Copy)\
                        .then_inc(t_ok, 1)

        @block.vector
        def _(v):
            L = lambda i: vlink(v, i)
            gate = lambda i, h, j: gateR[:, i, 3 * h + j:3 * h + j + 1]

            def tile_start(i):
                v.wait_ge(c_mm, 2 * i + 1)
                L(v.tensor_tensor(pc[:], ps[:, 6, 0:64].rearrange("p (h n) -> p h n", h=HEADS), cbias[:, i], ALU.add))
                L(v.tensor_reduce(cm[:], pc[:], AX.X, ALU.max))
                L(v.tensor_scalar(cm[:], cm[:], -1e20, None, ALU.max))
                L(v.tensor_tensor(pc[:], pc[:], cm[:].unsqueeze(2).broadcast_to((128, HEADS, NB_P)), ALU.subtract))
                v.sem_inc(c_a, 1)
                v.wait_ge(e_c, i + 1)
                L(v.tensor_reduce(cs[:], pc[:], AX.X, ALU.add))
                L(v.tensor_scalar(cs[:], cs[:], 1e-30, None, ALU.max))
                L(v.reciprocal(cs[:], cs[:]))
                L(v.tensor_tensor(cs[:], cs[:], gateR[:, i].rearrange("p (h j) -> p h j", j=3)[:, :, 0], ALU.mult))
                L(v.tensor_tensor(pc[:], pc[:], cs[:].unsqueeze(2).broadcast_to((128, HEADS, NB_P)), ALU.mult))
                v.sem_inc(c_v, 1)
                for h in range(HEADS):
                    n = 4 * i + h
                    v.wait_ge(i_rel, n + 1)
                    if h == 0:
                        if i >= 1:
                            v.wait_ge(selb_ok, i)
                        ins = v.tensor_scalar(score[:, 0:nk(i)], rel[:, n % 2, 0:nk(i)], wiR[:, i, h:h + 1], None, ALU.mult)
                    else:
                        ins = v.scalar_tensor_tensor(score[:, 0:nk(i)], rel[:, n % 2, 0:nk(i)], wiR[:, i, h:h + 1],
                                                     score[:, 0:nk(i)], ALU.mult, ALU.add)
                    L(ins)
                    v.sem_inc(i_use, 1)
                v.sem_inc(sc_ok, 1)

            def best(i, rounds):
                if i == 0:
                    return
                s = score[:, 0:nk(i)]
                for _ in range(rounds):
                    L(v.max(out=top8[:], in_=s))
                    L(v.match_replace(out=s, in_to_replace=top8[:], in_values=s, imm_value=-3e38))

            def select(i):
                s = score[:, 0:nk(i)]
                if i == 0:
                    v.wait_ge(sc_done, 1)
                    L(v.tensor_scalar(s, s, -1e29, BIG, ALU.is_lt, ALU.mult))
                else:
                    L(v.tensor_scalar(s, s, -2e38, BIG, ALU.is_gt, ALU.mult))
                v.sem_inc(sel_ok, 1)

            def biased(u):
                i, h, b = units[u]
                if b == DSA and h == 0:
                    v.wait_ge(selb_ok, i + 1)
                bias = selb[:, h, 0:nk(i)] if b == DSA else ali[:, 2 * h, 512 - nk(i):512]
                v.wait_ge(s_mm, u + 1)
                if u >= 3:
                    v.wait_ge(t_mm, u - 2)
                s = P[:, u % 3, 0:nk(i)]
                m = mx[:, u % 3:u % 3 + 1]
                L(v.tensor_tensor(s, ps[:, u % 2, 0:nk(i)], bias, ALU.add))
                v.tensor_reduce(m, s, AX.X, ALU.max, negate=True).then_inc(s_ok, 1)

            def scaled(u):
                i, h, b = units[u]
                v.wait_ge(e_ok, u + 1)
                r = rc[:, u % 3:u % 3 + 1]
                L(v.reciprocal(r, sm[:, u % 3:u % 3 + 1]))
                s = P[:, u % 3, 0:nk(i)]
                if b == DSA:
                    v.tensor_scalar(s, s, r, None, ALU.mult).then_inc(p_ok, 1)
                else:
                    v.tensor_scalar(s, s, r, gate(i, h, b), ALU.mult, ALU.mult).then_inc(p_ok, 1)

            def evacuate(u):
                i, h, b = units[u]
                g, _, last = group(u)
                if not last:
                    return
                hb = 64 * (h % 2)
                v.wait_ge(o_mm, u + 1)
                c = (4 if b == DSA else 2) + h // 2
                v.tensor_copy(mixT[hb:hb + 64, c, i * 128:(i + 1) * 128], ps[hb:hb + 64, 4 + g % 2, 0:128])\
                    .then_inc(o_ok, 1)

            v.wait_ge(cst_ok, 1)
            for u in range(N + 4):
                i = u // PER
                if u < N and u % PER == 0:
                    tile_start(i)
                if u < N:
                    biased(u)
                if 1 <= u <= N:
                    scaled(u - 1)
                if u < N and u % PER < 8:
                    if u % PER == 1:
                        v.wait_ge(sc_done, i + 1)
                    if u % PER >= 1:
                        best(i, (0, 2, 2, 2, 2, 2, 3, 3)[u % PER])
                    if u % PER == 7:
                        select(i)
                if u >= 3 and u - 3 < N:
                    evacuate(u - 3)


NPAIR = DEC // 2
JP, JW = PAST // 64 + 2, SEQ // 64 + 2
JI = PAST // 64 + 4
K_SEL_DEC = 256
N_SEL_BLK = PAST // 64 + 1
CMP = 0


def block_sample_attention(nc, io, G, ctx, sem, sbt):
    ps, ident, ones, mixT = G["ps"], G["ident"], G["ones"], G["mixT"]
    vlink, alink, plink = G["vlink"], G["alink"], G["plink"]
    kcT, vcR, gateR, wiR, qN, qD, qI, idx = (G[n] for n in ("kcT", "vcR", "gateR", "wiR", "qN", "qD", "qI", "blk_idx"))
    cache = sbt(ctx, "cache", [128, NPAIR, JP, 128])
    flat = sbt(ctx, "winidx", [128, NPAIR * JW * 128])
    win = flat[:].rearrange("p (t j x) -> p t j x", t=NPAIR, j=JW)
    keyi = flat[:, 0:NPAIR * JI * 32].rearrange("p (t j x) -> p t j x", t=NPAIR, j=JI)
    KT = sbt(ctx, "KTs", [128, 2, 512])
    room, used = [G["zA"][:].rearrange("p a n -> p (a n)"), G["zD"][:].rearrange("p a n -> p (a n)")], [0, 0]

    def scratch(side, rows, *shape):
        n = int(np.prod(shape))
        x = room[side][0:rows, used[side]:used[side] + n]
        used[side] += n
        if len(shape) == 1:
            return x
        names = "abcd"[:len(shape)]
        return x.rearrange("p (%s) -> p %s" % (" ".join(names), " ".join(names)), **dict(zip(names, shape)))

    S = scratch(0, 128, NPAIR, JP, 8)
    rows = scratch(0, DEC, PAST + 8)
    bias = scratch(1, 128, 2, JP, 8)
    biasW = scratch(1, 128, JW, 8)
    biasC = scratch(1, 128, 8)
    QB = scratch(1, 128, 2, NPAIR, 16)
    QIB = scratch(1, 128, NPAIR, 32)
    disti = scratch(1, 128, 3, JP)
    dist = scratch(1, 128, 3, JP)
    half = scratch(1, 128, 2)
    halfb = scratch(1, 128, 2)
    gw8 = scratch(1, DEC, DEC, 16)
    gw = scratch(1, 128, DEC, 16)
    wm = scratch(1, 128, NPAIR, 8)
    keyscore = scratch(1, 128, NPAIR, JI)
    vc2 = scratch(1, 128, NPAIR, HD)
    small = sbt(ctx, "as_small", [128, 12, 32])
    mxp, mrow, diag, sums = small[:, 0], small[:, 1, 0:1], small[0:32, 2], small[:, 3]
    rinv = small[:, 4:8]
    impT, blkm = small[:, 8, 0:NPAIR], small[:, 8, 8:8 + NPAIR]
    Pc = small[:, 9]
    acc, prod = small[0:64, 10], small[0:64, 11]
    imp = scratch(0, NPAIR, 2, 40)
    imp64 = scratch(0, NPAIR, 128)
    top8 = scratch(0, DEC, 8)
    disti = disti.bitcast(I32)
    scores_d = nc.dram_tensor("index_scores", (DEC, PAST + 1), F32, kind="Internal").ap()
    mask_d = nc.dram_tensor("index_mask", (DEC, PAST + 1), F32, kind="Internal").ap()

    s_new, idx_in, cache_in, win_in = sem("s_new"), sem("as_idx_in"), [sem("as_slc_in"), sem("as_dsa_in")], sem("as_win_in")
    idx_new, cache_new = sem("as_idx_new"), [sem("as_slc_new"), sem("as_dsa_new")]
    s_cst, s_zero, s_zero2, s_q = sem("as_cst"), sem("as_zero"), sem("as_zero2"), sem("as_q")
    k_t, k_ev, k_mm = sem("as_kt"), sem("as_kev"), sem("as_kmm")
    s_read, s_step, p_step, e_in, e_ok, pv_mm = (sem("as_" + n) for n in ("read", "vstep", "pstep", "ein", "eok", "pv"))
    ix_ok, ix_st, rows_in, mask_ok, mask_st, mask_in, new_in2 = (sem("as_" + n) for n in (
        "ix_ok", "ix_st", "rows_in", "mask_ok", "mask_st", "mask_in", "new2"))
    tiles_of = [NPAIR * JI // 4, NPAIR * JP // 2, NPAIR * JW // 2, NPAIR * JP // 2]
    first_chunk = [0]
    for n in tiles_of:
        first_chunk.append(first_chunk[-1] + n // 4)

    with nc.Block() as block:
        @block.sync
        def _(sp):
            sp.wait_ge(s_zero, 1)
            for a in range(2):
                sp.dma_start(keyi[64 * a:64 * a + 1, :, PAST // 64, :],
                             io["out16"][0, a::2, 0].unsqueeze(0)).then_inc(idx_new, 16)
                sp.dma_start(cache[64 * a:64 * a + 1, :, JP - 2, :],
                             io["out13"][0, a::2, 0].rearrange("s a d -> s (a d)").unsqueeze(0)).then_inc(cache_new[0], 16)
            sp.wait_ge(ix_ok, 1)
            for t in range(NPAIR):
                sp.dma_start(scores_d[2 * t:2 * t + 2, 0:PAST].rearrange("s (b j) -> s b j", j=32),
                             keyscore[:, t, 0:32]).then_inc(ix_st, 16)
                for a in range(2):
                    sp.dma_start(scores_d[2 * t + a:2 * t + a + 1, PAST:PAST + 1],
                                 keyscore[64 * a:64 * a + 1, t, 32:33]).then_inc(ix_st, 16)
            sp.wait_ge(ix_st, 16 * 3 * NPAIR)
            sp.dma_start(rows[:, 0:PAST + 1], scores_d).then_inc(rows_in, 16)
            sp.wait_ge(s_zero2, 1)
            for t in range(NPAIR):
                sp.dma_start(win[:, t, 0:8, :], io["state_nsa_win"][0, 2 * t:2 * t + 2]
                             .rearrange("s (b j) a d -> (s b) j (a d)", j=8)).then_inc(win_in, 16)
            for a in range(2):
                sp.dma_start(win[64 * a:64 * a + 1, :, 8, :],
                             io["out14"][0, a::2, 511].rearrange("s a d -> s (a d)").unsqueeze(0)).then_inc(win_in, 16)
            sp.wait_ge(pv_mm, 2)
            for a in range(2):
                sp.dma_start(cache[64 * a:64 * a + 1, :, JP - 2, :],
                             io["out15"][0, a::2, 0].rearrange("s a d -> s (a d)").unsqueeze(0)).then_inc(cache_new[1], 16)
            sp.wait_ge(mask_ok, 1)
            sp.dma_start(mask_d, rows[:, 0:PAST + 1]).then_inc(mask_st, 16)
            sp.wait_ge(mask_st, 16)
            for t in range(NPAIR):
                sp.dma_start(keyscore[:, t, 0:32], mask_d[2 * t:2 * t + 2, 0:PAST].rearrange("s (b j) -> s b j", j=32))\
                    .then_inc(mask_in, 16)
                for a in range(2):
                    sp.dma_start(keyscore[64 * a:64 * a + 1, t, 32:33], mask_d[2 * t + a:2 * t + a + 1, PAST:PAST + 1])\
                        .then_inc(mask_in, 16)

        @block.gpsimd
        def _(pool):
            g = nc.gpsimd
            L = lambda i: plink(pool, i)
            L(g.memset(keyi[:, :, PAST // 64:JI, :], 0.0))
            L(g.memset(cache[:, :, JP - 2:JP, :], 0.0))
            pool.sem_inc(s_zero, 1)

            def pages(dst, table, n_sem):
                for t in range(NPAIR):
                    g.indirect_dma_start(dst(t), None, table,
                                         bass.IndirectOffsetOnAxis(ap=idx[:, t:t + 1], axis=0)).then_inc(n_sem, 16)
            pages(lambda t: keyi[:, t, 0:32, :].rearrange("p j x -> p (j x)"),
                  io["cache_dsa_idx"][0].rearrange("n (s j) d -> (n s) (j d)", s=4), idx_in)
            pages(lambda t: cache[:, t, 0:32, :].rearrange("p j x -> p (j x)"),
                  io["cache_nsa_slc"][0].rearrange("n (s j) a d -> (n s) (j a d)", s=4), cache_in[0])
            L(g.iota(disti[:, 0, 0:32], pattern=[[-1, 32]], base=PAST, channel_multiplier=-32))
            L(g.iota(disti[:, 1, 0:8], pattern=[[-1, 8]], base=512, channel_multiplier=-8))
            L(g.iota(disti[:, 2, 0:1], pattern=[[0, 1]], base=PAST - 31, channel_multiplier=-32))
            L(g.memset(dist[:], 0.0))
            L(g.tensor_copy(dist[:, 0, 0:32], disti[:, 0, 0:32]))
            L(g.tensor_copy(dist[:, 1, 0:8], disti[:, 1, 0:8]))
            L(g.tensor_copy(dist[:, 2, 0:1], disti[:, 2, 0:1]))
            L(g.memset(half[:], 1.0))
            L(g.affine_select(out=half[:, 1:2], in_=half[:, 1:2], compare_op=ALU.is_ge, fill=0.0, base=-64,
                              pattern=[[0, 1]], channel_multiplier=1))
            L(g.tensor_scalar(half[:, 0:1], half[:, 1:2], -1.0, 1.0, ALU.mult, ALU.add))
            for i, (n, back) in enumerate(((32, 2048.0), (8, 512.0), (1, 2048.0))):
                L(g.tensor_scalar(halfb[:, 0:1], half[:, 1:2], back, None, ALU.mult))
                L(g.tensor_scalar(dist[:, i, 0:n], dist[:, i, 0:n], halfb[:, 0:1], None, ALU.add))
            L(g.tensor_scalar(halfb[:], half[:], 1.0, -BIG, ALU.subtract, ALU.mult))
            for h in range(HEADS):
                for a in range(2):
                    c = 4 * a + h
                    hb = halfb[:, a:a + 1]
                    L(g.tensor_scalar(bias[:, 0, :, c], dist[:, 0, :], -SLOPES[2 * h], hb, ALU.mult, ALU.add))
                    L(g.tensor_scalar(bias[:, 1, :, c], dist[:, 0, :], -SLOPES[2 * h + 1], hb, ALU.mult, ALU.add))
                    L(g.tensor_scalar(biasW[:, :, c], dist[:, 1, 0:JW], -SLOPES[2 * h], hb, ALU.mult, ALU.add))
                    L(g.tensor_scalar(biasC[:, c:c + 1], dist[:, 2, 0:1], -SLOPES[2 * h], hb, ALU.mult, ALU.add))
            for x, n in ((bias[:, 0], JP), (bias[:, 1], JP), (biasW, JW)):
                y = x[:, n - 2, :].rearrange("p (s h) -> p s h", s=2)
                L(g.affine_select(out=y, in_=y, compare_op=ALU.is_equal, fill=BIG, base=0,
                                  pattern=[[-64, 2], [0, 4]], channel_multiplier=1))
                L(g.memset(x[:, n - 1, :], BIG))
            pool.sem_inc(s_cst, 1)
            pool.wait_ge(k_mm, first_chunk[1])
            L(g.memset(win[:, :, JW - 2:JW, :], 0.0))
            pool.sem_inc(s_zero2, 1)
            pool.wait_ge(pv_mm, 2)
            pages(lambda t: cache[:, t, 0:32, :].rearrange("p j x -> p (j x)"),
                  io["cache_dsa_kv"][0].rearrange("n (s j) a d -> (n s) (j a d)", s=4), cache_in[1])

        @block.tensor
        def _(pe):
            step = [0]

            def take(n=1):
                step[0] += n
                pe.wait_ge(s_step, step[0])

            def keys(b, turn, product):
                n = tiles_of[b] // 4
                for c in range(n + 1):
                    g = first_chunk[b] + c
                    if c < n:
                        if g >= 2:
                            pe.wait_ge(k_ev, g - 1)
                        for u in range(4):
                            m = turn(4 * c + u, lambda q: ps[q, 4 + g % 2, u * 128:(u + 1) * 128])
                        m.then_inc(k_t, 1)
                    if c >= 1:
                        pe.wait_ge(k_ev, g)
                        for u in range(4):
                            m = product(4 * (c - 1) + u, KT[:, (g - 1) % 2, u * 128:(u + 1) * 128])
                        m.then_inc(k_mm, 1)

            def turn_index(n, out):
                t, j = divmod(n, JI // 4)
                return pe.transpose(out(slice(0, 128)), keyi[:, t, 4 * j:4 * j + 4, :].rearrange("p j x -> p (j x)"), ident[:])

            def product_index(n, k):
                t, j = divmod(n, JI // 4)
                return pe.matmul(ps[:, t, j * 32:(j + 1) * 32], k, QIB[:, t], start=True, stop=True)

            def turn_pair(src, J):
                def f(n, out):
                    t, j = divmod(n, J // 2)
                    pe.transpose(out(slice(0, 64)), src[:, t, 2 * j, 0:HD], ident[:])
                    return pe.matmul(out(slice(64, 128)), src[:, t, 2 * j + 1, 0:HD], ident[:], start=True, stop=True)
                return f

            def product_pair(q, J):
                def f(n, k):
                    t, j = divmod(n, J // 2)
                    return pe.matmul(ps[:, t, j * 16:(j + 1) * 16], k, QB[:, q, t], start=True, stop=True)
                return f

            def softmax_steps():
                take()
                pe.transpose(ps[0:32, 6, 0:128], mxp, ident[:]).then_inc(p_step, 1)
                take()
                pe.matmul(ps[:, 6, 128:160], ones[0:32, :], diag, start=True, stop=True).then_inc(p_step, 1)
                take()
                pe.matmul(ps[:, 6, 160:192], ones[:], sums, start=True, stop=True).then_inc(p_step, 1)

            def values(b, src, J):
                pe.wait_ge(e_ok, b + 1)
                for t in range(NPAIR):
                    for j in range(J - 1):
                        m = pe.matmul(ps[0:64, 7, b * 32 + 8 * t:b * 32 + 8 * t + 8], src[:, t, j, HD:128],
                                      S[:, t, j, :], start=(j == 0), stop=(j == J - 2))
                m.then_inc(pv_mm, 1)

            take()
            pe.matmul(ps[:, 6, 0:128], ones[0:DEC, :], gw8.rearrange("p a b -> p (a b)"), start=True, stop=True)\
                .then_inc(p_step, 1)
            pe.wait_ge(s_q, 1)
            pe.wait_ge(idx_in, 16 * NPAIR)
            pe.wait_ge(idx_new, 32)
            keys(0, turn_index, product_index)
            take()
            for t in range(NPAIR):
                m = pe.matmul(ps[:, 6, 256 + 8 * t:264 + 8 * t], kcT[:, 128 * t:128 * t + 128], QB[0:64, 0, t, 0:8],
                              start=True, stop=True)
            m.then_inc(p_step, 1)
            softmax_steps()
            pe.wait_ge(e_ok, 1)
            for t in range(NPAIR):
                m = pe.matmul(ps[0:64, 7, 8 * t:8 * t + 8], vc2[:, t], Pc[:, 8 * t:8 * t + 8], start=True, stop=True)
            m.then_inc(pv_mm, 1)
            take()
            pe.transpose(ps[0:NPAIR, 6, 0:128], impT, ident[:]).then_inc(p_step, 1)
            take()
            pe.transpose(ps[:, 6, 0:NPAIR], imp64, ident[0:NPAIR, 0:NPAIR]).then_inc(p_step, 1)
            pe.wait_ge(cache_in[0], 16 * NPAIR)
            pe.wait_ge(cache_new[0], 32)
            pe.wait_ge(s_read, 1)
            keys(1, turn_pair(cache, JP), product_pair(0, JP))
            softmax_steps()
            values(1, cache, JP)
            pe.wait_ge(win_in, 16 * (NPAIR + 2))
            pe.wait_ge(s_read, 2)
            keys(2, turn_pair(win, JW), product_pair(0, JW))
            softmax_steps()
            values(2, win, JW)
            pe.wait_ge(cache_in[1], 16 * NPAIR)
            pe.wait_ge(cache_new[1], 32)
            pe.wait_ge(s_read, 3)
            keys(3, turn_pair(cache, JP), product_pair(1, JP))
            softmax_steps()
            values(3, cache, JP)

        @block.scalar
        def _(act):
            def exp(b, x):
                act.wait_ge(e_in, b + 1)
                nc.scalar.activation(x, x, ACT.Exp).then_inc(e_ok, 1)

            def evacuate(b):
                for g in range(first_chunk[b], first_chunk[b + 1]):
                    act.wait_ge(k_t, g + 1)
                    if g >= 2:
                        act.wait_ge(k_mm, g - 1)
                    nc.scalar.activation(KT[:, g % 2, :], ps[:, 4 + g % 2, :], ACT.Copy).then_inc(k_ev, 1)

            evacuate(0)
            exp(0, Pc)
            evacuate(1)
            exp(1, S[:].rearrange("p t j c -> p (t j c)"))
            evacuate(2)
            exp(2, S[:, :, 0:JW, :].rearrange("p t j c -> p t (j c)"))
            evacuate(3)
            exp(3, S[:].rearrange("p t j c -> p (t j c)"))

        @block.vector
        def _(v):
            L = lambda i: vlink(v, i)
            TT = v.tensor_tensor
            step = [0]

            def give():
                v.sem_inc(s_step, 1)

            def take():
                step[0] += 1
                v.wait_ge(p_step, step[0])

            ROUNDS = K_SEL_DEC // 8

            def best(rounds):
                x = rows[:, 0:PAST + 1]
                for _ in range(rounds):
                    L(v.max(out=top8, in_=x))
                    L(v.match_replace(out=x, in_to_replace=top8, in_values=x, imm_value=-3e38))

            def softmax(b, x, J):
                c8 = lambda y: y.rearrange("p (t c) -> p t c", t=NPAIR)
                if J:
                    for t in range(NPAIR):
                        L(v.tensor_reduce(mxp[:, 8 * t:8 * t + 8], x[:, t].rearrange("p j c -> p c j"), AX.X, ALU.max))
                else:
                    L(v.tensor_copy(mxp, x))
                give()
                take()
                L(v.tensor_reduce(mrow[0:32], ps[0:32, 6, 0:128], AX.X, ALU.max))
                L(v.tensor_scalar(diag, ident[0:32, 0:32], mrow[0:32], None, ALU.mult))
                give()
                take()
                if J:
                    for t in range(NPAIR):
                        m = ps[:, 6, 128 + 8 * t:136 + 8 * t].unsqueeze(1).broadcast_to((128, J, 8))
                        L(TT(x[:, t], x[:, t], m, ALU.subtract))
                else:
                    L(TT(x, x, ps[:, 6, 128:160], ALU.subtract))
                v.sem_inc(e_in, 1)
                v.wait_ge(e_ok, b + 1)
                if J:
                    for t in range(NPAIR):
                        L(v.tensor_reduce(sums[:, 8 * t:8 * t + 8], x[:, t].rearrange("p j c -> p c j"), AX.X, ALU.add))
                else:
                    L(v.tensor_copy(sums, x))
                give()
                take()
                L(v.reciprocal(rinv[:, b], ps[:, 6, 160:192]))

            L(TT(gw8[:, :, 0:12], gateR[0:DEC, NT].unsqueeze(1).broadcast_to((DEC, DEC, 12)),
                 ident[0:DEC, 0:DEC].unsqueeze(2).broadcast_to((DEC, DEC, 12)), ALU.mult))
            L(TT(gw8[:, :, 12:16], wiR[0:DEC, NT].unsqueeze(1).broadcast_to((DEC, DEC, 4)),
                 ident[0:DEC, 0:DEC].unsqueeze(2).broadcast_to((DEC, DEC, 4)), ALU.mult))
            give()
            L(v.memset(QB[:], 0.0))
            L(v.memset(QIB[:], 0.0))
            for a in range(2):
                for t in range(NPAIR):
                    for i, q in enumerate((qN, qD)):
                        L(v.tensor_copy(QB[64 * a:64 * a + 64, i, t, 8 * a:8 * a + 8].rearrange("p (s h) -> p s h", s=2),
                                        q[:, :, SEQ + 2 * t:SEQ + 2 * t + 2].rearrange("d h s -> d s h")))
            for a in range(4):
                for t in range(NPAIR):
                    L(v.tensor_copy(QIB[32 * a:32 * a + 32, t, 8 * a:8 * a + 8].rearrange("p (s h) -> p s h", s=2),
                                    qI[:, :, SEQ + 2 * t:SEQ + 2 * t + 2].rearrange("d h s -> d s h")))
            v.sem_inc(s_q, 1)
            for a in range(2):
                L(v.tensor_copy(vc2[64 * a:64 * a + 64], vcR[:, a:DEC:2, :]))
            take()
            L(v.tensor_copy(gw.rearrange("p a b -> p (a b)"), ps[:, 6, 0:128]))
            give()
            v.wait_ge(s_cst, 1)
            for a in range(2):
                L(v.tensor_scalar(wm[:, :, 4 * a:4 * a + 4], gw[:, a:DEC:2, 12:16], half[:, a:a + 1], None, ALU.mult))
            v.wait_ge(k_mm, first_chunk[1])
            for t in range(NPAIR):
                x = S[:, t].rearrange("p j c -> p (j c)")
                for j0, j1 in ((0, 32), (32, 34)):
                    L(v.scalar_tensor_tensor(S[:, t, j0:j1], ps[:, t, 8 * j0:8 * j1].rearrange("p (j c) -> p j c", c=8), 0.0,
                                             wm[:, t].unsqueeze(1).broadcast_to((128, j1 - j0, 8)), ALU.max, ALU.mult))
                L(v.tensor_reduce(keyscore[:, t, 0:JP], S[:, t], AX.X, ALU.add))
            v.sem_inc(ix_ok, 1)
            v.sem_inc(s_read, 1)
            take()
            L(TT(Pc.rearrange("p (t c) -> p t c", t=NPAIR), ps[:, 6, 256:288].rearrange("p (t c) -> p t c", t=NPAIR),
                 biasC.unsqueeze(1).broadcast_to((128, NPAIR, 8)), ALU.add))
            softmax(0, Pc, 0)
            L(TT(mxp, Pc, rinv[:, 0], ALU.mult))
            L(v.tensor_reduce(impT, mxp.rearrange("p (t c) -> p t c", t=NPAIR), AX.X, ALU.add))
            give()
            take()
            L(v.tensor_copy(imp64, ps[0:NPAIR, 6, 0:128]))
            L(v.tensor_reduce(imp[:, :, 0:32], imp64.rearrange("p (s b r) -> p s b r", s=2, r=2), AX.X, ALU.add))
            L(v.memset(imp[:, :, 0:1], 1e4))
            L(v.memset(imp[:, :, 31:33], 1e4))
            for a in range(2):
                x = imp[:, a, 0:N_SEL_BLK]
                for _ in range(2):
                    L(v.max(out=top8[0:NPAIR], in_=x))
                    L(v.match_replace(out=x, in_to_replace=top8[0:NPAIR], in_values=x, imm_value=-1.0))
            L(v.tensor_scalar(imp[:, :, 0:32], imp[:, :, 0:32], 0.0, BIG, ALU.is_ge, ALU.mult))
            i64 = imp64.rearrange("p (s b r) -> p s b r", s=2, r=2)
            for r in range(2):
                L(v.tensor_copy(i64[:, :, :, r], imp[:, :, 0:32]))
            give()
            take()
            L(v.tensor_copy(blkm, ps[:, 6, 0:NPAIR]))
            v.wait_ge(rows_in, 16)
            L(v.memset(keyscore[:, :, 32:JP], 0.0))
            best(11)
            v.wait_ge(k_mm, first_chunk[2])
            for t in range(NPAIR):
                L(v.scalar_tensor_tensor(S[:, t].rearrange("p j c -> p (j c)"), ps[:, t, 0:8 * JP], blkm[:, t:t + 1],
                                         bias[:, 0].rearrange("p j c -> p (j c)"), ALU.add, ALU.add))
            v.sem_inc(s_read, 1)
            softmax(1, S, JP)
            best(9)
            v.wait_ge(k_mm, first_chunk[3])
            v.wait_ge(pv_mm, 2)
            for t in range(NPAIR):
                L(TT(S[:, t, 0:JW].rearrange("p j c -> p (j c)"), ps[:, t, 0:8 * JW],
                     biasW.rearrange("p j c -> p (j c)"), ALU.add))
            v.sem_inc(s_read, 1)
            softmax(2, S[:, :, 0:JW, :], JW)
            best(ROUNDS - 20)
            x = rows[:, 0:PAST + 1]
            L(v.tensor_scalar(x, x, -2e38, BIG, ALU.is_gt, ALU.mult))
            v.sem_inc(mask_ok, 1)
            v.wait_ge(mask_in, 16 * 3 * NPAIR)
            v.wait_ge(k_mm, first_chunk[4])
            v.wait_ge(pv_mm, 3)
            for t in range(NPAIR):
                L(TT(S[:, t], ps[:, t, 0:8 * JP].rearrange("p (j c) -> p j c", c=8), bias[:, 1], ALU.add))
                L(TT(S[:, t], S[:, t], keyscore[:, t, 0:JP].unsqueeze(2).broadcast_to((128, JP, 8)), ALU.add))
            softmax(3, S, JP)
            v.wait_ge(pv_mm, 4)
            gates = lambda b: gw[0:64, :, b:12:3]
            for b in range(4):
                y = (acc if b in (0, 3) else prod)
                L(TT(y, ps[0:64, 7, 32 * b:32 * b + 32], rinv[0:64, b], ALU.mult))
                if b < 3:
                    L(TT(y.rearrange("p (s h) -> p s h", h=4), y.rearrange("p (s h) -> p s h", h=4), gates(b), ALU.mult))
                if b in (1, 2):
                    L(TT(acc, acc, prod, ALU.add))
                if b >= 2:
                    for h in range(HEADS):
                        hb = 64 * (h % 2)
                        L(v.tensor_copy(mixT[hb:hb + 64, (2 if b == 2 else 4) + h // 2, SEQ:NTOK], acc[:, h:32:4]))


SLOTS = 128
MAX_CH = (NTOK * TOPK + E * SLOTS) // SLOTS
MAX_N = -(-NTOK // SLOTS)
AHEAD = MAX_N
NR = NT + 1


def block_out_router(nc, io, G, ctx, sem, sbt):
    ps, ident, ones, mixT = G["ps"], G["ident"], G["ones"], G["mixT"]
    vlink, alink, plink = G["vlink"], G["alink"], G["plink"]
    slot_i, gateW, GT, tab, rowtok, biasT = (G[n] for n in ("slot_i", "gateW", "GT", "tab", "rowtok", "biasT"))
    w_out = sbt(ctx, "w_out_s", [128, KD, D])
    xin = sbt(ctx, "xin", [128, NR, D])
    modP = sbt(ctx, "modP", [128, 3, D])
    modS = sbt(ctx, "modS", [DEC, 3, D])
    ln1 = sbt(ctx, "ln1", [128, 2, D])
    h2 = sbt(ctx, "h2", [128, 2, D])
    h2T = sbt(ctx, "h2T", [128, 2, KD, 128])
    wr = sbt(ctx, "wr", [128, KD, E])
    br = sbt(ctx, "br", [128, E])
    bgu = sbt(ctx, "bgu", [E, 2 * FF])
    st = sbt(ctx, "st7", [128, 2, 6])
    mv = sbt(ctx, "mv7", [128, 2])
    rstd = sbt(ctx, "rstd7", [128, 1])
    logits = sbt(ctx, "logits", [128, NR, E])
    w_o_in = [sem("r_w_o0"), sem("r_w_o1")]
    w_in_, x_in7, c_in7, o_mm, o_rd, var7, rs7 = (sem("r_" + n) for n in ("w_in", "x_in", "c_in", "o_mm", "o_rd", "var", "rs"))
    h_ok, t_mm, t_ev, l_mm, x1_st, b_mm = (sem("r_" + n) for n in (
        "h_ok", "t_mm", "t_ev", "l_mm", "x1_st", "b_mm"))
    h2_st = [sem("r_h2_st0"), sem("r_h2_st1")]
    x1_ok, g_cst, a_ok, rv, rp, ra = (sem("r_" + n) for n in ("x1_ok", "g_cst", "a_ok", "rv", "rp", "ra"))
    strict = sbt(ctx, "strict", [128, 128])
    ioti = sbt(ctx, "ioti", [128, 128], I32)
    iot = sbt(ctx, "iot", [128, 128])
    toki = sbt(ctx, "toki", [128, NR], I32)
    tokf = sbt(ctx, "tokf", [128, NR])
    valid = sbt(ctx, "valid", [128, NR])
    rev = sbt(ctx, "rev", [128, E])
    oh = sbt(ctx, "oh", [128, TOPK, NR, E])
    tmp = sbt(ctx, "tmp7", [128, NR, E])
    tops = sbt(ctx, "tops", [128, TOPK, NR])
    col = sbt(ctx, "col7", [128, NR])
    T1 = sbt(ctx, "T1", [128, NR, E])
    Gd = sbt(ctx, "Gd", [128, NR, E])
    thr = sbt(ctx, "thr", [128, E, MAX_N])
    edge = sbt(ctx, "edge", [128, MAX_CH + 1])
    nch = sbt(ctx, "nch", [128, E + 2])
    cum = sbt(ctx, "cum", [128, 2, E + 2])
    slotf = sbt(ctx, "slotf", [128, TOPK, NR])
    GE = sbt(ctx, "GE", [128, TOPK, NR, MAX_CH + 1])
    HI = sbt(ctx, "HI", [128, TOPK, NR, MAX_CH])
    lo = sbt(ctx, "lo", [128, TOPK, NR])
    LO = sbt(ctx, "LO", [128, 2, NR, SLOTS])
    order = [NT] + list(range(NT))

    def rows_of(t):
        return 128 if t < NT else DEC

    with nc.Block() as block:
        @block.sync
        def _(sp):
            for a in range(2):
                sp.dma_start(w_out[:, :, a * 512:(a + 1) * 512], io["w_out"][0, :, a * 512:(a + 1) * 512]
                             .rearrange("(k p) n -> p k n", p=128)).then_inc(w_o_in[a], 16)
            sp.dma_start(xin[:, 0:NT, :], io["x_prompt"][0].rearrange("(t p) d -> p t d", p=128)).then_inc(x_in7, 16)
            sp.dma_start(xin[0:DEC, NT, :], io["x_sample"].rearrange("b s d -> (b s) d")).then_inc(x_in7, 16)
            md = G["mod_dram"]
            sp.dma_start(modP[:], bass.AP(md.tensor, 2 * D, [[0, 128], [D, 3], [1, D]])).then_inc(c_in7, 16)
            sp.dma_start(modS[:], md[1:9, 2 * D:5 * D].rearrange("s (a d) -> s a d", a=3)).then_inc(c_in7, 16)
            for i, n in enumerate(("ln1_g", "ln1_b")):
                sp.dma_start(ln1[:, i], bass.AP(io[n].tensor, 0, [[0, 128], [1, D]])).then_inc(c_in7, 16)
            sp.dma_start(wr[:], io["moe_wr"][0].rearrange("(k p) n -> p k n", p=128)).then_inc(w_in_, 16)
            sp.dma_start(br[:], bass.AP(io["moe_br"].tensor, 0, [[0, 128], [1, E]])).then_inc(w_in_, 16)
            sp.dma_start(bgu[:], io["moe_bgu"][0]).then_inc(w_in_, 16)
            for s, t in enumerate(order):
                r = rows_of(t)
                sp.wait_ge(x1_ok, s + 1)
                sp.dma_start(G["x2_dram"][t * 128:t * 128 + r], xin[0:r, t]).then_inc(x1_st, 16)
                sp.wait_ge(h_ok, s + 1)
                sp.dma_start(G["h2_dram"][t * 128:t * 128 + r], h2[0:r, s % 2]).then_inc(h2_st[s % 2], 16)
            sp.wait_ge(x1_st, 16 * NR)
            sp.wait_ge(h2_st[0], 16 * ((NR + 1) // 2))
            sp.wait_ge(h2_st[1], 16 * (NR // 2))

        @block.tensor
        def _(pe):
            def out_proj(s):
                t = order[s]
                r = rows_of(t)
                if s >= 2:
                    pe.wait_ge(o_rd, s - 1)
                for a in range(2):
                    if s == 0:
                        pe.wait_ge(w_o_in[a], 16)
                    for k in range(KD):
                        m = pe.matmul(ps[0:r, 2 * (s % 2) + a, :], mixT[:, k, t * 128:t * 128 + r],
                                      w_out[:, k, a * 512:(a + 1) * 512], start=(k == 0), stop=(k == KD - 1))
                m.then_inc(o_mm, 1)

            def router(s):
                t = order[s]
                r = rows_of(t)
                pe.wait_ge(h_ok, s + 1)
                if s >= 1:
                    pe.wait_ge(t_ev, s)
                for k in range(KD):
                    m = pe.transpose(ps[:, 4 + k // 4, (k % 4) * 128:(k % 4) * 128 + r],
                                     h2[0:r, s % 2, k * 128:(k + 1) * 128], ident[0:r, 0:r])
                m.then_inc(t_mm, 1)
                pe.wait_ge(t_ev, s + 1)
                for k in range(KD):
                    m = pe.matmul(ps[0:r, 6, t * E:(t + 1) * E], h2T[:, s % 2, k, 0:r], wr[:, k, :],
                                  start=(k == 0), stop=(k == KD - 1))
                m.then_inc(l_mm, 1)

            out_proj(0)
            out_proj(1)
            pe.wait_ge(w_in_, 48)
            for c in range(2 * FF // 128):
                m = pe.transpose(ps[:, 7, c * E:(c + 1) * E], bgu[:, c * 128:(c + 1) * 128], ident[0:E, 0:E])
            m.then_inc(b_mm, 1)
            for s in range(NR):
                router(s)
                if s + 2 < NR:
                    out_proj(s + 2)
            pe.wait_ge(rv, 1)
            for t in range(NR):
                for j in range(t + 1):
                    m = pe.matmul(ps[:, 0, t * E:(t + 1) * E], (strict if j == t else ones)[:], T1[:, j],
                                  start=(j == 0), stop=(j == t))
            for j in range(NR):
                m = pe.matmul(ps[:, 1, 0:E], ones[:], T1[:, j], start=(j == 0), stop=(j == NR - 1))
            for t in range(NR):
                r = rows_of(t)
                m = pe.transpose(ps[0:E, 2 + t // 4, (t % 4) * 128:(t % 4) * 128 + r], Gd[0:r, t], ident[0:r, 0:r])
            m.then_inc(rp, 1)
            for k in range(TOPK):
                pe.wait_ge(rv, 2 + k)
                for t in range(NR):
                    m = pe.matmul(ps[0:SLOTS, 4, 0:MAX_CH], LO[:, k % 2, t], HI[:, k, t], start=(k == 0 and t == 0),
                                  stop=(k == TOPK - 1 and t == NR - 1))
                m.then_inc(rp, 1)

        @block.scalar
        def _(act):
            for s, t in enumerate(order):
                r = rows_of(t)
                for i in range(2):
                    act.wait_ge(var7, 2 * s + i + 1)
                    act.activation(rstd[0:r], mv[0:r, 1:2], ACT.Sqrt).then_inc(rs7, 1)
                act.wait_ge(t_mm, s + 1)
                act.activation(h2T[:, s % 2, :, 0:r], ps[:, 4:6, :].rearrange("p b (k t) -> p (b k) t", k=4)[:, :, 0:r],
                               ACT.Copy).then_inc(t_ev, 1)
            act.wait_ge(a_ok, 1)
            act.activation(tops[:], tops[:], ACT.Exp).then_inc(ra, 1)

        @block.gpsimd
        def _(pool):
            g = nc.gpsimd
            L = lambda i: plink(pool, i)
            L(g.memset(strict[:], 1.0))
            L(g.affine_select(out=strict[:], in_=strict[:], compare_op=ALU.is_gt, fill=0.0, base=0,
                              pattern=[[1, 128]], channel_multiplier=-1))
            L(g.iota(ioti[:], pattern=[[1, 128]], base=0, channel_multiplier=0))
            L(g.tensor_copy(iot[:], ioti[:]))
            L(g.iota(toki[:], pattern=[[128, NR]], base=0, channel_multiplier=1))
            L(g.tensor_copy(tokf[:], toki[:]))
            L(g.memset(valid[:], 1.0))
            L(g.affine_select(out=valid[:], in_=valid[:], compare_op=ALU.is_gt, fill=0.0, base=NTOK,
                              pattern=[[-128, NR]], channel_multiplier=-1))
            L(g.tensor_scalar(rev[:], iot[:, 0:E], -1.0, float(E), ALU.mult, ALU.add))
            L(g.memset(logits[:], 0.0))
            pool.sem_inc(g_cst, 1)

        @block.vector
        def _(v):
            L = lambda i: vlink(v, i)
            TT = v.tensor_tensor

            def norm(x, r, n):
                for i in range(2):
                    L(v.bn_stats(st[0:r, i], x[:, i * 512:(i + 1) * 512]))
                L(v.bn_aggr(mv[0:r], st[0:r].rearrange("p a b -> p (a b)")))
                L(v.tensor_scalar(mv[0:r, 1:2], mv[0:r, 1:2], 1e-5, None, ALU.add))
                v.sem_inc(var7, 1)
                v.wait_ge(rs7, n + 1)
                L(v.reciprocal(rstd[0:r], rstd[0:r]))

            v.wait_ge(c_in7, 64)
            v.wait_ge(x_in7, 32)
            for s, t in enumerate(order):
                r = rows_of(t)
                m = modP if t < NT else modS
                x, hh = xin[0:r, t], h2[0:r, s % 2]
                v.wait_ge(o_mm, s + 1)
                if s >= 2:
                    v.wait_ge(h2_st[s % 2], 16 * (s // 2))
                L(TT(hh.rearrange("p (a n) -> p a n", a=2), ps[0:r, 2 * (s % 2):2 * (s % 2) + 2, :],
                     m[0:r, 0].rearrange("p (a n) -> p a n", a=2), ALU.mult))
                v.sem_inc(o_rd, 1)
                L(v.scalar_tensor_tensor(x, x, DN_ALPHA, hh, ALU.mult, ALU.add))
                norm(x, r, 2 * s)
                L(v.scalar_tensor_tensor(x, x, mv[0:r, 0:1], ln1[0:r, 0], ALU.subtract, ALU.mult))
                L(v.scalar_tensor_tensor(x, x, rstd[0:r], ln1[0:r, 1], ALU.mult, ALU.add))
                v.sem_inc(x1_ok, 1)
                norm(x, r, 2 * s + 1)
                L(v.scalar_tensor_tensor(hh, x, mv[0:r, 0:1], m[0:r, 2], ALU.subtract, ALU.mult))
                L(v.scalar_tensor_tensor(hh, hh, rstd[0:r], m[0:r, 1], ALU.mult, ALU.add))
                v.sem_inc(h_ok, 1)
            v.wait_ge(b_mm, 1)
            bT = biasT[:].rearrange("p e (q s c) -> p e q s c", q=4, s=2)
            for q in range(4):
                for i in range(2):
                    c = 8 * i + 2 * q
                    L(v.tensor_copy(bT[:, :, q, i], ps[:, 7, c * E:(c + 2) * E].rearrange("p (c e) -> p e c", e=E)))
            v.wait_ge(g_cst, 1)
            v.wait_ge(l_mm, NR)
            bb = br[:].unsqueeze(1)
            L(TT(logits[:, 0:NT], ps[:, 6, 0:NT * E].rearrange("p (t e) -> p t e", e=E),
                 bb.broadcast_to((128, NT, E)), ALU.add))
            L(TT(logits[0:DEC, NT], ps[0:DEC, 6, NT * E:NR * E], br[0:DEC], ALU.add))
            e_ = lambda x: x.unsqueeze(2).broadcast_to((128, NR, E))
            for k in range(TOPK):
                L(v.tensor_reduce(tops[:, k], logits[:], AX.X, ALU.max))
                L(TT(tmp[:], logits[:], e_(tops[:, k]), ALU.is_equal))
                L(TT(tmp[:], tmp[:], rev[:].unsqueeze(1).broadcast_to((128, NR, E)), ALU.mult))
                L(v.tensor_reduce(col[:], tmp[:], AX.X, ALU.max))
                L(TT(oh[:, k], rev[:].unsqueeze(1).broadcast_to((128, NR, E)), e_(col[:]), ALU.is_equal))
                L(v.scalar_tensor_tensor(logits[:].rearrange("p t e -> p (t e)"), oh[:, k].rearrange("p t e -> p (t e)"),
                                         -3e38, logits[:].rearrange("p t e -> p (t e)"), ALU.mult, ALU.add))
            for k in range(TOPK - 1, -1, -1):
                L(TT(tops[:, k], tops[:, k], tops[:, 0], ALU.subtract))
            v.sem_inc(a_ok, 1)
            L(TT(T1[:], oh[:, 0], oh[:, 1], ALU.add))
            for k in (2, 3):
                L(TT(T1[:], T1[:], oh[:, k], ALU.add))
            L(TT(T1[:], T1[:], e_(valid[:]), ALU.mult))
            v.wait_ge(ra, 1)
            L(v.tensor_reduce(col[:], tops[:].rearrange("p k t -> p t k"), AX.X, ALU.add))
            L(v.reciprocal(col[:], col[:]))
            L(TT(tops[:], tops[:], col[:].unsqueeze(1).broadcast_to((128, TOPK, NR)), ALU.mult))
            L(v.tensor_copy(gateW[:], tops[:].rearrange("p k t -> p t k")))
            L(TT(Gd[:], oh[:, 0], e_(tops[:, 0]), ALU.mult))
            for k in (1, 2, 3):
                L(TT(tmp[:], oh[:, k], e_(tops[:, k]), ALU.mult))
                L(TT(Gd[:], Gd[:], tmp[:], ALU.add))
            v.sem_inc(rv, 1)
            v.wait_ge(rp, 1)
            L(v.tensor_copy(GT[:, 0:512], ps[0:E, 2, :]))
            L(v.tensor_copy(GT[:, SEQ:NTOK], ps[0:E, 3, 0:DEC]))
            cnt = ps[:, 1, 0:E]
            L(v.tensor_scalar(thr[:], iot[:, 0:MAX_N].unsqueeze(1).broadcast_to((128, E, MAX_N)),
                              float(SLOTS), None, ALU.mult))
            L(TT(thr[:], thr[:], cnt.unsqueeze(2).broadcast_to((128, E, MAX_N)), ALU.is_lt))
            L(v.tensor_reduce(nch[:, 0:E], thr[:], AX.X, ALU.add))
            L(v.tensor_scalar(nch[:, 0:E], nch[:, 0:E], 1.0, None, ALU.max))
            L(v.memset(cum[:], 0.0))
            L(v.tensor_copy(cum[:, 0, 1:E + 1], nch[:, 0:E]))
            a = 0
            for d in (1, 2, 4, 8, 16, 32):
                L(v.tensor_copy(cum[:, 1 - a, 0:d], cum[:, a, 0:d]))
                if d < E + 1:
                    L(TT(cum[:, 1 - a, d:E + 1], cum[:, a, d:E + 1], cum[:, a, 0:E + 1 - d], ALU.add))
                a = 1 - a
            F = cum[:, a, 0:E + 1]
            L(v.tensor_copy(tab[0:1, 0, 0:E + 1], F[0:1]))
            L(v.tensor_copy(tab[0:1, 1, 0:E], nch[0:1, 0:E]))
            L(v.memset(tab[0:1, 1, E:E + 1], 1))
            L(v.tensor_scalar(nch[:, 0:E], F[:, 0:E], float(SLOTS), None, ALU.mult))
            L(TT(T1[:], ps[:, 0, 0:NR * E].rearrange("p (t e) -> p t e", e=E),
                 nch[:, 0:E].unsqueeze(1).broadcast_to((128, NR, E)), ALU.add))
            for k in range(TOPK):
                L(TT(tmp[:], oh[:, k], T1[:], ALU.mult))
                L(v.tensor_reduce(slotf[:, k], tmp[:], AX.X, ALU.add))
            L(v.tensor_copy(slot_i[:], slotf[:].rearrange("p k t -> p t k")))
            L(v.tensor_scalar(edge[:], iot[:, 0:MAX_CH + 1], float(SLOTS), None, ALU.mult))
            kt = lambda x: x.rearrange("p k t b -> p (k t) b")
            sl = slotf[:].rearrange("p k t -> p (k t)")
            L(TT(kt(GE[:]), edge[:].unsqueeze(1).broadcast_to((128, TOPK * NR, MAX_CH + 1)),
                 sl.unsqueeze(2).broadcast_to((128, TOPK * NR, MAX_CH + 1)), ALU.is_le))
            L(TT(kt(HI[:]), kt(GE[:])[:, :, 0:MAX_CH], kt(GE[:])[:, :, 1:MAX_CH + 1], ALU.subtract))
            L(v.tensor_reduce(lo[:].rearrange("p k t -> p (k t)"), kt(GE[:]), AX.X, ALU.add))
            lf = lo[:].rearrange("p k t -> p (k t)")
            L(v.tensor_scalar(lf, lf, -1.0, -float(SLOTS), ALU.add, ALU.mult))
            L(TT(lf, lf, sl, ALU.add))
            L(TT(tokf[:], tokf[:], valid[:], ALU.mult))
            for k in range(TOPK):
                L(TT(HI[:, k], HI[:, k], tokf[:].unsqueeze(2).broadcast_to((128, NR, MAX_CH)), ALU.mult))
                if k >= 2:
                    v.wait_ge(rp, k)
                L(TT(LO[:, k % 2], iot[:, 0:SLOTS].unsqueeze(1).broadcast_to((128, NR, SLOTS)),
                     lo[:, k].unsqueeze(2).broadcast_to((128, NR, SLOTS)), ALU.is_equal))
                v.sem_inc(rv, 1)
            v.wait_ge(rp, 1 + TOPK)
            L(v.memset(rowtok[:, MAX_CH:MAX_CH + AHEAD], 0))
            L(v.tensor_copy(rowtok[:, 0:MAX_CH], ps[0:SLOTS, 4, 0:MAX_CH]))


XR = 8
assert XR >= AHEAD + 1
NXG = 3
NQ = 4


def block_experts(nc, io, G, ctx, sem, sbt):
    ps, ident, tab, rowtok, biasT = (G[n] for n in ("ps", "ident", "tab", "rowtok", "biasT"))
    plink = G["plink"]
    wgu = sbt(ctx, "wgu", [128, NQ, KD, 2, 256])
    wd = sbt(ctx, "wd", [128, NQ, KD, 256])
    xg = sbt(ctx, "xg", [SLOTS, NXG, D])
    gidx = sbt(ctx, "gidx", [SLOTS, 1], I32)
    xT = sbt(ctx, "xTm", [128, KD, XR * SLOTS])
    aT = sbt(ctx, "aT", [128, KD, MAX_N * SLOTS])
    dT = sbt(ctx, "dT", [128, KD, SLOTS])
    hx = sbt(ctx, "hx", [128, 4, SLOTS])
    sg = sbt(ctx, "sg", [128, 2, SLOTS])
    orow = sbt(ctx, "orow", [SLOTS, D])
    zero = sbt(ctx, "zero_m", [128, D])
    zero_ok = sem("m_zero_ok")
    gu_in = [sem(f"m_gu_in{i}") for i in range(NQ)]
    d_in = [sem(f"m_d_in{i}") for i in range(NQ)]
    pe_go, pool_go = sem("m_pe_go"), sem("m_pool_go")
    x_in = [sem(f"m_x_in{i}") for i in range(NXG)]
    x_idx, x_t, x_ev = sem("m_x_idx"), sem("m_x_t"), sem("m_x_ev")
    gu_mm, gu_rd, sg_in, sg_ok, a_ok = (sem("m_" + n) for n in ("gu_mm", "gu_rd", "sg_in", "sg_ok", "a_ok"))
    sg_v, sg_w = sem("m_sg_v"), sem("m_sg_w")
    d_mm, d_rd, r_t, r_ev, r_st, act_go = (sem("m_" + n) for n in ("d_mm", "d_rd", "r_t", "r_ev", "r_st", "act_go"))

    def expert_loop(eng, body):
        with eng.Fori(0, E) as e:
            F0 = eng.value_load(tab[0:1, 0, ds(e, 1)], min_val=0, max_val=MAX_CH)
            N = eng.value_load(tab[0:1, 1, ds(e, 1)], min_val=1, max_val=MAX_N)
            body(e, F0, N)

    def passes(eng, F0, N, body):
        for p in range(NQ):
            with eng.Fori(0, N) as j:
                body(p, F0 * NQ + N * p + j, j)

    with nc.Block() as block:
        @block.sync
        def _(sp):
            def weights(e, F0=None, N=None):
                for p in range(NQ):
                    if F0 is not None:
                        sp.wait_ge(gu_mm, F0 * NQ + N * (p + 1))
                    for s in range(2):
                        sp.dma_start(wgu[:, p, :, s], io["moe_wgu"][0, ds(e, 1), :, s * FF + p * 256:s * FF + p * 256 + 256]
                                     .rearrange("a (k p) n -> p (a k) n", p=128)).then_inc(gu_in[p], 16)
                    if F0 is None and p == 0:
                        sp.wait_ge(x_in[(AHEAD - 1) % NXG], 16 * ((AHEAD - 1) // NXG + 1))
                for p in range(NQ):
                    if F0 is not None:
                        sp.wait_ge(d_mm, (F0 + N) * NQ)
                    sp.dma_start(wd[:, p], io["moe_wd"][0, ds(e, 1), :, p * 256:p * 256 + 256]
                                 .rearrange("a (k p) n -> p (a k) n", p=128)).then_inc(d_in[p], 16)
            weights(0)
            with sp.Fori(1, E) as e:
                weights(e, sp.value_load(tab[0:1, 0, ds(e - 1, 1)], min_val=0, max_val=MAX_CH),
                        sp.value_load(tab[0:1, 1, ds(e - 1, 1)], min_val=1, max_val=MAX_N))

        @block.gpsimd
        def _(pool):
            total = pool.value_load(tab[0:1, 0, E:E + 1], min_val=E, max_val=MAX_CH)

            def gather(buf, idx):
                nc.gpsimd.indirect_dma_start(xg[:, buf], None, G["h2_dram"], bass.IndirectOffsetOnAxis(ap=idx, axis=0))\
                    .then_inc(x_in[buf], 16)
            for g in range(AHEAD):
                if g >= NXG:
                    pool.wait_ge(x_t, g - NXG + 1)
                gather(g % NXG, rowtok[:, g:g + 1])
            with pool.Fori(AHEAD, total + AHEAD) as g:
                pool.wait_ge(x_t, g)
                nc.gpsimd.tensor_copy(gidx[:], rowtok[:, ds(g, 1)]).then_inc(x_idx, 1)
                pool.wait_ge(x_idx, g - AHEAD + 1)
                pool.sem_inc(pool_go, 1)
                gather(0, gidx[:, 0:1])

        @block.tensor
        def _(pe):
            def turn(buf, k0=0, k1=KD):
                for k in range(k0, k1):
                    m = pe.transpose(ps[:, 4 + k // 4, (k % 4) * SLOTS:(k % 4 + 1) * SLOTS], xg[:, buf, k * 128:(k + 1) * 128],
                                     ident[:])
                if k1 == KD:
                    m.then_inc(x_t, 1)

            for g in range(AHEAD):
                pe.wait_ge(x_in[g % NXG], 16 * (g // NXG + 1))
                if g >= 1:
                    pe.wait_ge(x_ev, g)
                turn(g % NXG)

            def expert(e, F0, N):
                def gate_up(p, q, j):
                    pe.wait_ge(gu_rd, q + 1)
                    c = ((F0 + j) % XR) * SLOTS
                    b = (q % 2) * 512
                    x = ps[:].rearrange("p b n -> p (b n)")
                    for i in range(4):
                        for k in range(KD):
                            m = pe.matmul(x[:, ds(b + i * SLOTS, SLOTS)], wgu[:, p, k, i // 2, (i % 2) * 128:(i % 2 + 1) * 128],
                                          xT[:, k, ds(c, SLOTS)], start=(k == 0), stop=(k == KD - 1))
                    m.then_inc(gu_mm, 1)

                def down(p, q, j):
                    pe.wait_ge(d_rd, q + 1)
                    for i in range(2):
                        for k in range(KD):
                            if p == 0 and i == 0 and k == KD - 2:
                                pe.wait_ge(a_ok, (F0 + N) * NQ)
                                pe.sem_inc(pe_go, 1)
                            m = pe.matmul(ps[:, 2 + p % 2, i * SLOTS:(i + 1) * SLOTS], wd[:, p, k, i * 128:(i + 1) * 128],
                                          aT[:, k, ds(j * SLOTS, SLOTS)], start=(k == 0), stop=(k == KD - 1))
                    m.then_inc(d_mm, 1)

                pe.wait_ge(x_ev, F0 + N)
                pe.sem_inc(pe_go, 1)
                for p in range(NQ):
                    pe.wait_ge(gu_in[p], 32 * e + 32)
                    pe.sem_inc(pe_go, 1)
                    with pe.Fori(0, N) as j:
                        gate_up(p, F0 * NQ + N * p + j, j)
                prefetch(e)
                for p in range(NQ):
                    pe.wait_ge(d_in[p], 16 * e + 16)
                pe.sem_inc(pe_go, 1)
                with pe.Fori(0, N) as j:
                    pe.wait_ge(x_in[0], 16 * (F0 + j + 1 + -(-AHEAD // NXG)))
                    pe.wait_ge(x_ev, F0 + j + AHEAD)
                    pe.sem_inc(pe_go, 1)
                    turn(0, 0, KD // 2)
                    pe.wait_ge(a_ok, F0 * NQ + N * (NQ - 1))
                    pe.sem_inc(pe_go, 1)
                    for p in range(NQ):
                        down(p, (F0 + j) * NQ + p, j)
                    turn(0, KD // 2, KD)
                    pe.wait_ge(r_ev, F0 + j + 1)
                    for k in range(KD):
                        if k % 2 == 0:
                            pe.wait_ge(d_rd, (F0 + j) * NQ + k // 2 + 3)
                            pe.sem_inc(pe_go, 1)
                        m = pe.transpose(ps[0:SLOTS, 6 + k // 4, (k % 4) * 128:(k % 4 + 1) * 128], dT[:, k, :], ident[:])
                    m.then_inc(r_t, 1)
            regs = [nc.alloc_registers(f"expert_{n}", engines=[pe.engine]) for n in ("first", "chunks")]

            def prefetch(e):
                nc.regs_mov(regs[0], pe.value_load(tab[0:1, 0, ds(e + 1, 1)], min_val=0, max_val=MAX_CH))
                nc.regs_mov(regs[1], pe.value_load(tab[0:1, 1, ds(e + 1, 1)], min_val=1, max_val=MAX_CH))
            nc.regs_mov(regs[0], pe.value_load(tab[0:1, 0, 0:1], min_val=0, max_val=MAX_CH))
            nc.regs_mov(regs[1], pe.value_load(tab[0:1, 1, 0:1], min_val=1, max_val=MAX_N))
            with pe.Fori(0, E) as e:
                expert(e, nc.snap(regs[0], min_val=0, max_val=MAX_CH), nc.snap(regs[1], min_val=1, max_val=MAX_N))

        @block.scalar
        def _(act):
            act.sem_inc(d_rd, 2)
            total = act.value_load(tab[0:1, 0, E:E + 1], min_val=E, max_val=MAX_CH)
            act.wait_ge(zero_ok, 1)
            act.dma_start(G["outbuf"][(MAX_CH + 1) * SLOTS:(MAX_CH + 2) * SLOTS, :], zero[:]).then_inc(r_st, 16)
            def turned(g):
                nc.scalar.activation(xT[:, :, ds((g % XR) * SLOTS, SLOTS)], ps[:, 4:6, :].rearrange("p b (k t) -> p (b k) t", k=4),
                                     ACT.Copy).then_inc(x_ev, 1)

            for g in range(AHEAD):
                act.wait_ge(x_t, g + 1)
                turned(g)

            def expert(e, F0, N):
                def sigmoid(p, q, j):
                    act.wait_ge(sg_in, q + 1)
                    nc.scalar.activation(sg[:], hx[:, 0:2], ACT.Sigmoid, scale=1.702).then_inc(sg_ok, 1)

                passes(act, F0, N, sigmoid)
                with act.Fori(0, N) as j:
                    for p in range(NQ):
                        act.wait_ge(d_mm, (F0 + j) * NQ + p + 1)
                        nc.scalar.activation(dT[:, 2 * p:2 * p + 2, :], ps[:, 2 + p % 2, 0:2 * SLOTS].rearrange("p (a n) -> p a n", a=2),
                                             ACT.Copy).then_inc(d_rd, 1)
                    act.wait_ge(x_t, F0 + j + AHEAD + 1)
                    turned(F0 + j + AHEAD)
                    act.wait_ge(r_ev, F0 + j + 2)
                    act.dma_start(G["outbuf"][ds((F0 + j) * SLOTS, SLOTS), :], orow[:]).then_inc(r_st, 16)

            expert_loop(act, expert)
            total = act.value_load(tab[0:1, 0, E:E + 1], min_val=E, max_val=MAX_CH)
            act.wait_ge(r_st, total * 16 + 16)
            act.sem_inc(act_go, 1)

        @block.vector
        def _(v):
            TT = v.tensor_tensor
            v.sem_inc(gu_rd, 2)
            v.memset(zero[:], 0.0).then_inc(zero_ok, 1)
            v.sem_inc(r_ev, 1)

            def expert(e, F0, N):
                def activate(p, q, j):
                    link = [0]

                    def L(ins):
                        link[0] += 1
                        ins.then_inc(sg_v, 1)
                        v.wait_ge(sg_v, q * 3 + link[0])
                    x = ps[:].rearrange("p b n -> p (b n)")[:, ds((q % 2) * 512, 4 * SLOTS)].rearrange("p (a n) -> p a n", a=4)
                    b = biasT[:, ds(e, 1), 4 * p:4 * p + 4].rearrange("p a c -> p (a c)").unsqueeze(2).broadcast_to((128, 4, SLOTS))
                    v.wait_ge(gu_mm, q + 1)
                    L(TT(hx[:], x, b, ALU.add))
                    L(v.tensor_scalar(hx[:], hx[:], 7.0, None, ALU.min))
                    v.sem_inc(gu_rd, 1)
                    v.sem_inc(sg_in, 1)
                    L(v.tensor_scalar(hx[:, 2:4], hx[:, 2:4], -7.0, 1.0, ALU.max, ALU.add))
                    v.wait_ge(sg_ok, q + 1)
                    TT(hx[:, 2:4], hx[:, 2:4], hx[:, 0:2], ALU.mult).then_inc(sg_w, 1)
                    v.wait_ge(sg_w, q + 1)
                    TT(aT[:, 2 * p:2 * p + 2, ds(j * SLOTS, SLOTS)], hx[:, 2:4], sg[:], ALU.mult).then_inc(a_ok, 1)
                    v.wait_ge(a_ok, q + 1)
                passes(v, F0, N, activate)
                with v.Fori(0, N) as j:
                    v.wait_ge(r_t, F0 + j + 1)
                    v.wait_ge(r_st, 16 * (F0 + j) + 16)
                    v.tensor_copy(orow[:].rearrange("p (a n) -> p a n", a=2), ps[0:SLOTS, 6:8, :]).then_inc(r_ev, 1)
            expert_loop(v, expert)


def block_combine(nc, io, G, ctx, sem, sbt):
    ps, vlink = G["ps"], G["vlink"]
    slot_i, gateW, GT = G["slot_i"], G["gateW"], G["GT"]
    x1 = sbt(ctx, "x1", [128, NR, D])
    rowsg = sbt(ctx, "rowsg", [128, NR, TOPK, D])
    g2P = sbt(ctx, "g2P", [128, D])
    g2S = sbt(ctx, "g2S", [DEC, D])
    ln2 = sbt(ctx, "ln2", [128, 2, D])
    bd = sbt(ctx, "bd", [E, D])
    st = sbt(ctx, "st9", [128, 2, 6])
    mv = sbt(ctx, "mv9", [128, 2])
    rstd = sbt(ctx, "rstd9", [128, 1])
    x_in9, c_in9, b_in9, y_mm, y_rd, var9, rs9, out_ok, out_st = (sem("f_" + n) for n in (
        "x_in", "c_in", "b_in", "y_mm", "y_rd", "var", "rs", "out_ok", "out_st"))
    g_in = [sem(f"f_g_in{s}") for s in range(NR)]
    order = [NT] + list(range(NT))

    def rows_of(t):
        return 128 if t < NT else DEC

    with nc.Block() as block:
        @block.sync
        def _(sp):
            sp.dma_start(bd[:], io["moe_bd"][0]).then_inc(b_in9, 16)
            sp.dma_start(x1[0:DEC, NT, :], G["x2_dram"][SEQ:NTOK]).then_inc(x_in9, 16)
            sp.dma_start(x1[:, 0:NT, :], G["x2_dram"][0:SEQ].rearrange("(t p) d -> p t d", p=128)).then_inc(x_in9, 16)
            md = G["mod_dram"]
            sp.dma_start(g2P[:], bass.AP(md.tensor, 5 * D, [[0, 128], [1, D]])).then_inc(c_in9, 16)
            sp.dma_start(g2S[:], md[1:9, 5 * D:6 * D]).then_inc(c_in9, 16)
            for i, n in enumerate(("ln2_g", "ln2_b")):
                sp.dma_start(ln2[:, i], bass.AP(io[n].tensor, 0, [[0, 128], [1, D]])).then_inc(c_in9, 16)
            for s, t in enumerate(order):
                sp.wait_ge(out_ok, s + 1)
                if t < NT:
                    sp.dma_start(io["out0"][0, t * 128:(t + 1) * 128], x1[:, t]).then_inc(out_st, 16)
                else:
                    sp.dma_start(io["out1"].rearrange("b s d -> (b s) d"), x1[0:DEC, t]).then_inc(out_st, 16)
            sp.wait_ge(out_st, 16 * NR)

        @block.gpsimd
        def _(pool):
            for s, t in enumerate(order):
                r = rows_of(t)
                for k in range(TOPK):
                    nc.gpsimd.indirect_dma_start(rowsg[0:r, s, k], None, G["outbuf"][0:(MAX_CH + 1) * SLOTS],
                                                 bass.IndirectOffsetOnAxis(ap=slot_i[0:r, t, k:k + 1], axis=0))\
                        .then_inc(g_in[s], 16)

        @block.tensor
        def _(pe):
            pe.wait_ge(b_in9, 16)
            for s, t in enumerate(order):
                r = rows_of(t)
                if s >= 2:
                    pe.wait_ge(y_rd, s - 1)
                for a in range(2):
                    m = pe.matmul(ps[0:r, 2 * (s % 2) + a, :], GT[:, t * 128:t * 128 + r], bd[:, a * 512:(a + 1) * 512],
                                  start=True, stop=True)
                m.then_inc(y_mm, 1)

        @block.scalar
        def _(act):
            for s, t in enumerate(order):
                act.wait_ge(var9, s + 1)
                act.activation(rstd[0:rows_of(t)], mv[0:rows_of(t), 1:2], ACT.Sqrt).then_inc(rs9, 1)

        @block.vector
        def _(v):
            L = lambda i: vlink(v, i)
            v.wait_ge(x_in9, 32)
            v.wait_ge(c_in9, 64)
            for s, t in enumerate(order):
                r = rows_of(t)
                x = x1[0:r, t]
                y = rowsg[0:r, s, 0]
                half2 = lambda z: z.rearrange("p (a n) -> p a n", a=2)
                v.wait_ge(y_mm, s + 1)
                v.wait_ge(g_in[s], 16 * TOPK)
                L(v.scalar_tensor_tensor(half2(y), half2(y), gateW[0:r, t, 0:1], ps[0:r, 2 * (s % 2):2 * (s % 2) + 2, :],
                                         ALU.mult, ALU.add))
                v.sem_inc(y_rd, 1)
                for k in range(1, TOPK):
                    L(v.scalar_tensor_tensor(y, rowsg[0:r, s, k], gateW[0:r, t, k:k + 1], y, ALU.mult, ALU.add))
                L(v.tensor_tensor(y, y, (g2P if t < NT else g2S)[0:r], ALU.mult))
                L(v.scalar_tensor_tensor(x, x, DN_ALPHA, y, ALU.mult, ALU.add))
                for i in range(2):
                    L(v.bn_stats(st[0:r, i], x[:, i * 512:(i + 1) * 512]))
                L(v.bn_aggr(mv[0:r], st[0:r].rearrange("p a b -> p (a b)")))
                L(v.tensor_scalar(mv[0:r, 1:2], mv[0:r, 1:2], 1e-5, None, ALU.add))
                v.sem_inc(var9, 1)
                v.wait_ge(rs9, s + 1)
                L(v.reciprocal(rstd[0:r], rstd[0:r]))
                L(v.scalar_tensor_tensor(x, x, mv[0:r, 0:1], ln2[0:r, 0], ALU.subtract, ALU.mult))
                L(v.scalar_tensor_tensor(x, x, rstd[0:r], ln2[0:r, 1], ALU.mult, ALU.add))
                v.sem_inc(out_ok, 1)




_OUTS = [
    ((1, 512, 1024), "float32"), ((8, 1, 1024), "float32"),
    ((1, 1, 4, 64, 64), "float32"), ((1, 1, 896), "float32"),
    ((1, 1, 512, 2, 64), "float32"), ((1, 1, 512, 2, 64), "float32"), ((1, 1, 512, 2, 64), "float32"),
    ((1, 1, 512, 2, 64), "float32"), ((1, 1, 512, 32), "float32"), ((1, 1, 2, 256), "float32"),
    ((1, 8, 4, 64, 64), "float32"), ((1, 8, 896), "float32"),
    ((1, 8, 1, 2, 64), "float32"), ((1, 8, 1, 2, 64), "float32"), ((1, 8, 512, 2, 64), "float32"),
    ((1, 8, 1, 2, 64), "float32"), ((1, 8, 1, 32), "float32"), ((1, 8, 2, 256), "float32"),
]


def kernel(**inputs):
    import concourse.bacc as _bacc
    from concourse.bass_utils import run_bass_kernel_spmd as _run

    nc = _bacc.Bacc("TRN2", target_bir_lowering=False, num_devices=1)
    arrays, io = {}, {}
    for name, a in inputs.items():
        a = np.ascontiguousarray(a)
        arrays[f"in_{name}"] = a
        io[name] = nc.dram_tensor(f"in_{name}", a.shape, mybir.dt.from_np(a.dtype), kind="ExternalInput").ap()
    for i, (shape, dtype) in enumerate(_OUTS):
        io[f"out{i}"] = nc.dram_tensor(f"out_{i}", shape, mybir.dt.from_np(np.dtype(dtype)),
                                       kind="ExternalOutput").ap()
    build(nc, io)
    r = _run(nc, [arrays], core_ids=[0])
    return tuple(r.results[0][f"out_{i}"] for i in range(len(_OUTS)))
```
